# Optimizing a Trainium2 kernel written in Bass

```python
import jax, jax.numpy as jnp
from jax import lax
import numpy as np

D_MODEL = 1024
BATCH = 1
SEQ = 512
DEPTH = 2
DEC_BATCH = 8
DEC_SEQ = 1
PAST_LEN = 2048
PAGE_SIZE = 128

N_A = DEPTH // 2
N_B = DEPTH - N_A
PLE_DIM = 256
EPS = 1e-6
GLA_HEADS = 4
GLA_DK = D_MODEL // 2
GLA_DV = D_MODEL
GLA_HK = GLA_DK // GLA_HEADS
GLA_HV = GLA_DV // GLA_HEADS
GATE_RANK = 16
GATE_NORM = 16.0
CHUNK = 64
GLA_IN = 2 * GLA_DK + 2 * GLA_DV + GATE_RANK
SB_HEADS = 16
SB_HD = D_MODEL // SB_HEADS
SB_WIDTH = SB_HEADS * SB_HD
Q_BLOCK = 128
SB_BIAS_INIT = -8.0

kernel_name = 'yoco_gla_stickbreaking_step'

def rms_norm(x, g):
    xf = x.astype(jnp.float32)
    y = xf * lax.rsqrt(jnp.mean(xf * xf, axis=-1, keepdims=True) + EPS)
    return (y * g.astype(jnp.float32)).astype(x.dtype)

def gla_chunked(q, k, v, gk, s0):
    B, L, H, DK = q.shape
    DV = v.shape[-1]
    c = min(CHUNK, L)
    n = -(-L // c)
    pad = n * c - L

    def prep(a):
        a = jnp.pad(a.astype(jnp.float32), ((0, 0), (0, pad), (0, 0), (0, 0)))
        return a.reshape(B, n, c, H, a.shape[-1]).transpose(0, 3, 1, 2, 4)

    qc, kc, vc, gc = prep(q), prep(k), prep(v), prep(gk)
    b = jnp.cumsum(gc, axis=3)
    b_last = b[:, :, :, -1:, :]
    q_in = qc * jnp.exp(b)
    k_in = kc * jnp.exp(-b)
    causal = jnp.tril(jnp.ones((c, c), dtype=bool))
    att = jnp.where(causal, jnp.einsum('bhnik,bhnjk->bhnij', q_in, k_in), 0.0)
    o_intra = jnp.einsum('bhnij,bhnjv->bhniv', att, vc)
    chunk_kv = jnp.einsum('bhnck,bhncv->bhnkv', kc * jnp.exp(b_last - b), vc)
    decay = jnp.exp(b_last[:, :, :, 0, :])
    if s0 is None:
        s0 = jnp.zeros((B, H, DK, DV), jnp.float32)

    def step(s, inp):
        dcy, kv = inp
        return dcy[..., None] * s + kv, s

    s_final, s_starts = lax.scan(step, s0.astype(jnp.float32),
                                 (jnp.moveaxis(decay, 2, 0), jnp.moveaxis(chunk_kv, 2, 0)))
    s_starts = jnp.moveaxis(s_starts, 0, 2)
    o_inter = jnp.einsum('bhnck,bhnkv->bhncv', q_in, s_starts)
    o = (o_intra + o_inter).transpose(0, 2, 3, 1, 4).reshape(B, n * c, H, DV)[:, :L]
    return o, s_final

def gla_mixer(hn, w_in, w_gk2, b_gk, g_out, w_out, s0):
    B, L, _ = hn.shape
    proj = hn @ w_in
    i1, i2 = GLA_DK, 2 * GLA_DK
    i3, i4 = i2 + GLA_DV, i2 + 2 * GLA_DV
    q = proj[..., :i1].reshape(B, L, GLA_HEADS, GLA_HK) * (GLA_HK ** -0.5)
    k = proj[..., i1:i2].reshape(B, L, GLA_HEADS, GLA_HK)
    v = proj[..., i2:i3].reshape(B, L, GLA_HEADS, GLA_HV)
    g = proj[..., i3:i4]
    gk = jax.nn.log_sigmoid((proj[..., i4:] @ w_gk2 + b_gk).astype(jnp.float32)) / GATE_NORM
    gk = gk.reshape(B, L, GLA_HEADS, GLA_HK)
    o, s = gla_chunked(q, k, v, gk, s0)
    o = rms_norm(o, g_out).astype(hn.dtype).reshape(B, L, GLA_DV) * jax.nn.silu(g)
    return o @ w_out, s

def stick_breaking(q, k, v, bias, q_pos, k_pos):
    B, Lq, H, D = q.shape
    qb = min(Q_BLOCK, Lq)
    nb = -(-Lq // qb)
    pad = nb * qb - Lq
    qblocks = jnp.pad(q, ((0, 0), (0, pad), (0, 0), (0, 0))).reshape(B, nb, qb, H, D).transpose(1, 0, 2, 3, 4)
    pblocks = jnp.pad(q_pos, (0, pad)).reshape(nb, qb)
    scale = D ** -0.5
    bias_f = bias.astype(jnp.float32)[None, :, None, None]

    def one_block(args):
        qblk, pos = args
        z = jnp.einsum('bqhd,bkhd->bhqk', qblk, k).astype(jnp.float32) * scale + bias_f
        mask = k_pos[None, :] < pos[:, None]
        log_keep = jnp.where(mask, jax.nn.log_sigmoid(-z), 0.0)
        later = lax.cumsum(log_keep, axis=3, reverse=True) - log_keep
        a = jnp.where(mask, jnp.exp(jax.nn.log_sigmoid(z) + later), 0.0)
        return jnp.einsum('bhqk,bkhd->bqhd', a.astype(v.dtype), v)

    out = lax.map(one_block, (qblocks, pblocks))
    return out.transpose(1, 0, 2, 3, 4).reshape(B, nb * qb, H, D)[:, :Lq]

def sb_mixer(hn, w_in, bias, w_out, k_all, v_all, q_pos, k_pos):
    B, L, _ = hn.shape
    proj = hn @ w_in
    q = proj[..., :SB_WIDTH].reshape(B, L, SB_HEADS, SB_HD)
    g = proj[..., SB_WIDTH:]
    o = stick_breaking(q, k_all, v_all, bias, q_pos, k_pos).reshape(B, L, SB_WIDTH) * jax.nn.silu(g)
    return o @ w_out

def shared_kv(h, g_kv, w_kv):
    B, L, _ = h.shape
    kv = rms_norm(h, g_kv) @ w_kv
    k = kv[..., :SB_WIDTH].reshape(B, L, SB_HEADS, SB_HD)
    v = kv[..., SB_WIDTH:].reshape(B, L, SB_HEADS, SB_HD)
    return k, v

def ple_add(h, p_i, g, w_gate, w_up):
    gate = jax.nn.sigmoid(rms_norm(h, g) @ w_gate)
    return h + gate * (p_i @ w_up)

def run_group(x, p, gla_s0, k_past, v_past, g_pre, w_ple_gate, w_ple_up, g_ple,
              gla_w_in, gla_w_gk2, gla_b_gk, gla_g_out, gla_w_out,
              g_kv, w_kv, sb_w_in, sb_bias, sb_w_out, g_final):
    L = x.shape[1]
    past = 0 if k_past is None else k_past.shape[1]
    q_pos = past + jnp.arange(L, dtype=jnp.int32)
    k_pos = jnp.arange(past + L, dtype=jnp.int32)
    h = x
    states = []
    k_new = v_new = k_all = v_all = None
    for i in range(DEPTH):
        hn = rms_norm(h, g_pre[i])
        if i < N_A:
            s0 = None if gla_s0 is None else gla_s0[i]
            out, s = gla_mixer(hn, gla_w_in[i], gla_w_gk2[i], gla_b_gk[i], gla_g_out[i], gla_w_out[i], s0)
            states.append(s.astype(x.dtype))
        else:
            j = i - N_A
            out = sb_mixer(hn, sb_w_in[j], sb_bias[j], sb_w_out[j], k_all, v_all, q_pos, k_pos)
        h = h + out
        h = ple_add(h, p[i], g_ple[i], w_ple_gate[i], w_ple_up[i])
        if i == N_A - 1:
            k_new, v_new = shared_kv(h, g_kv, w_kv)
            if k_past is None:
                k_all, v_all = k_new, v_new
            else:
                k_all = jnp.concatenate([k_past.astype(k_new.dtype), k_new], axis=1)
                v_all = jnp.concatenate([v_past.astype(v_new.dtype), v_new], axis=1)
    return rms_norm(h, g_final), jnp.stack(states), k_new, v_new

def setup_inputs(seed: int = 0) -> dict:
    key = jax.random.key(seed)
    ks = jax.random.split(key, 24)
    n_pages = PAST_LEN // PAGE_SIZE
    n_pool = (DEC_BATCH * n_pages * 5) // 4

    def nrm(k, shape, scale=1.0):
        return jax.random.normal(k, shape, jnp.float32) * scale

    perm = jax.random.permutation(ks[5], n_pool)[:DEC_BATCH * n_pages]
    page_table = perm.reshape(DEC_BATCH, n_pages).astype(jnp.int32)
    return {
        'x_prompt': nrm(ks[0], (BATCH, SEQ, D_MODEL)),
        'x_sample': nrm(ks[1], (DEC_BATCH, DEC_SEQ, D_MODEL)),
        'state_gla': nrm(ks[2], (N_A, DEC_BATCH, GLA_HEADS, GLA_HK, GLA_HV), 0.3),
        'cache_k': nrm(ks[3], (n_pool, PAGE_SIZE, SB_HEADS, SB_HD)),
        'cache_v': nrm(ks[4], (n_pool, PAGE_SIZE, SB_HEADS, SB_HD)),
        'page_table': page_table,
        'p_prompt': nrm(ks[6], (DEPTH, BATCH, SEQ, PLE_DIM)),
        'p_sample': nrm(ks[7], (DEPTH, DEC_BATCH, DEC_SEQ, PLE_DIM)),
        'g_pre': 1.0 + nrm(ks[8], (DEPTH, D_MODEL), 0.05),
        'w_ple_gate': nrm(ks[9], (DEPTH, D_MODEL, D_MODEL), D_MODEL ** -0.5),
        'w_ple_up': nrm(ks[10], (DEPTH, PLE_DIM, D_MODEL), 0.5 * PLE_DIM ** -0.5),
        'g_ple': 1.0 + nrm(ks[11], (DEPTH, D_MODEL), 0.05),
        'gla_w_in': nrm(ks[12], (N_A, D_MODEL, GLA_IN), D_MODEL ** -0.5),
        'gla_w_gk2': nrm(ks[13], (N_A, GATE_RANK, GLA_DK), GATE_RANK ** -0.5),
        'gla_b_gk': nrm(ks[14], (N_A, GLA_DK), 0.1),
        'gla_g_out': 1.0 + nrm(ks[15], (N_A, GLA_HV), 0.05),
        'gla_w_out': nrm(ks[16], (N_A, GLA_DV, D_MODEL), 0.5 * GLA_DV ** -0.5),
        'g_kv': 1.0 + nrm(ks[17], (D_MODEL,), 0.05),
        'w_kv': nrm(ks[18], (D_MODEL, 2 * SB_WIDTH), D_MODEL ** -0.5),
        'sb_w_in': nrm(ks[19], (N_B, D_MODEL, 2 * SB_WIDTH), D_MODEL ** -0.5),
        'sb_bias': SB_BIAS_INIT + nrm(ks[22], (N_B, SB_HEADS), 0.3),
        'sb_w_out': nrm(ks[20], (N_B, SB_WIDTH, D_MODEL), 0.5 * SB_WIDTH ** -0.5),
        'g_final': 1.0 + nrm(ks[21], (D_MODEL,), 0.05),
    }

def reference(x_prompt, x_sample, state_gla, cache_k, cache_v, page_table, p_prompt, p_sample,
              g_pre, w_ple_gate, w_ple_up, g_ple, gla_w_in, gla_w_gk2, gla_b_gk, gla_g_out, gla_w_out,
              g_kv, w_kv, sb_w_in, sb_bias, sb_w_out, g_final):
    weights = (g_pre, w_ple_gate, w_ple_up, g_ple, gla_w_in, gla_w_gk2, gla_b_gk, gla_g_out, gla_w_out,
               g_kv, w_kv, sb_w_in, sb_bias, sb_w_out, g_final)
    y_prompt, state_gla_prompt, k_prompt, v_prompt = run_group(x_prompt, p_prompt, None, None, None, *weights)
    db, n_pages = page_table.shape
    k_past = cache_k[page_table].reshape(db, n_pages * PAGE_SIZE, SB_HEADS, SB_HD)
    v_past = cache_v[page_table].reshape(db, n_pages * PAGE_SIZE, SB_HEADS, SB_HD)
    y_sample, state_gla_sample, k_sample, v_sample = run_group(x_sample, p_sample, state_gla, k_past, v_past, *weights)
    return (y_prompt, y_sample, state_gla_prompt, state_gla_sample, k_prompt, v_prompt, k_sample, v_sample)


_drawn_inputs = setup_inputs


def setup_inputs(seed=0):
    import zlib

    import numpy as np

    out = dict(_drawn_inputs(seed))
    spreads = {}
    factors = {'cache_k': 8.0,
     'cache_v': 7.744,
     'g_ple': 8.0,
     'gla_g_out': 4.168,
     'sb_w_in': 8.0,
     'sb_bias': 8.0,
     'sb_w_out': 7.562}
    for name, (base, spread) in spreads.items():
        noise = np.random.default_rng([zlib.crc32(name.encode()), seed]).standard_normal(out[name].shape)
        drawn = base * np.exp(spread * noise) if base else spread * noise
        out[name] = __import__('jax').numpy.asarray(drawn.astype(out[name].dtype))
    for name, factor in factors.items():
        out[name] = (out[name] * factor).astype(out[name].dtype)
    return out
```

```python
import concourse.bass as bass
from concourse import mybir
from contextlib import ExitStack

F32 = mybir.dt.float32
F32R = mybir.dt.float32r
BF16 = mybir.dt.bfloat16
I32 = mybir.dt.int32
ALU = mybir.AluOpType
ACT = mybir.ActivationFunctionType
AX = mybir.AxisListType

P = 128
D = 1024
KT = D // P
NP_TOK = 512
NS = 8
T = NP_TOK + NS
H2 = T // 2
TB = NP_TOK // P
PLE = 256
EPS = 1e-6
GH, HK, HV = 4, 128, 256
CH = 64
NCH = NP_TOK // CH
RANK = 16
GATE_NORM = 16.0
SH, HD = 16, 64
NPG = 16
PAST = P * NPG
NPAGES = NS * NPG
NEG = -1e30

PHASES = {}
_j = _m = 0
for _name, _n, _per in (("gk", 2, 1), ("q", 4, 1), ("k", 4, 1), ("v", 8, 1), ("g", 8, 1), ("up0", 2, 4),
                        ("wo0", 8, 1), ("ple0", 8, 1), ("q1", 8, 1), ("g1", 8, 1), ("K", 8, 1), ("V", 8, 1),
                        ("up1", 2, 4), ("wo1", 8, 1), ("ple1", 8, 1)):
    PHASES[_name] = (_j, _n, _m)
    _j += _n
    _m += 1 if _name == "gk" else _n * _per
NJOBS = _j
GFINAL, GOUT, BGK, NVEC = 40, 48, 50, 54
GAIN = {"gk": 0, "q": 0, "k": 0, "v": 0, "g": 0, "up0": None, "wo0": GOUT, "ple0": 16, "q1": 8, "g1": 8,
        "K": 32, "V": 32, "up1": None, "wo1": None, "ple1": 24}
K_PER_JOB = 5
POOL_SHARE = (0, 2, 4)
RING = 6
ZB = {0: (0, 0), 2: (0, P), 1: (1, 0), 3: (2, 0)}
PSEG = {0: 0, 2: 128, 1: 512, 3: 768}
SEG = {0: 0, 2: 129, 1: 514, 3: 771}
NZ = P * (1 + 2 + 3 + 4)
AB = {0: (3, 0), 1: (4, 0), 2: (5, 0), 3: (5, 256)}
AO = {0: 0, 1: 512, 2: 896, 3: 1152}


def phase_of(job):
    for name, (j0, n, m0) in PHASES.items():
        if j0 <= job < j0 + n:
            return name
    raise ValueError(job)


def tiles_through(job):
    if job < PHASES["q"][0]:
        return 1
    name = phase_of(job)
    j0, _, m0 = PHASES[name]
    return m0 + (job - j0 + 1) * (4 if name[:2] == "up" else 1)


def gains_through(pair):
    return sum(GAIN[phase_of(2 * p)] is not None for p in range(pair + 1))


def pool_pages(n):
    return sum(i % 5 in POOL_SHARE for i in range(n))


class Steps:

    def __init__(self, engine, sem):
        self.engine, self.sem, self.n = engine, sem, 0

    def did(self, ins):
        self.n += 1
        ins.then_inc(self.sem, 1)

    def wait(self):
        self.engine.wait_ge(self.sem, self.n)

    def then(self, ins):
        self.did(ins)
        self.wait()


def build(nc, x_prompt, x_sample, state_gla, cache_k, cache_v, page_table, p_prompt, p_sample,
          g_pre, w_ple_gate, w_ple_up, g_ple, gla_w_in, gla_w_gk2, gla_b_gk, gla_g_out, gla_w_out,
          g_kv, w_kv, sb_w_in, sb_bias, sb_w_out, g_final,
          y_prompt, y_sample, st_prompt, st_sample, k_prompt, v_prompt, k_sample, v_sample):
    with ExitStack() as ctx:
        top = [(nc.sbuf_base + 63) // 64 * 64]

        def at(name, shape, dt, offset):
            return nc.alloc_sbuf_tensor_at(name, shape, dt, offset=offset)

        def size(shape, dt=F32):
            n = 2 if dt == BF16 else 4
            for s in shape[1:]:
                n *= s
            return (n + 63) // 64 * 64

        def new(name, shape, dt=F32):
            t = at(name, shape, dt, top[0])
            top[0] += size(shape, dt)
            assert top[0] <= nc.sbuf_usable_end, (name, top[0] - nc.sbuf_usable_end)
            return t

        hT = new("hT", [P, KT, T])
        offA = top[0]
        xa_hi, xa_lo = new("xa_hi", [P, KT, T], F32R), new("xa_lo", [P, KT, T], F32R)
        offB = top[0]
        xb_hi, xb_lo = new("xb_hi", [P, KT, T], F32R), new("xb_lo", [P, KT, T], F32R)
        w_raw = new("w_raw", [P, 2, 2048])
        w_hi = [new(f"w_hi{i}", [P, 1024], F32R) for i in range(2)]
        w_lo = [new(f"w_lo{i}", [P, 1024], F32R) for i in range(2)]
        work = new("work", [P, 4, T])
        sqacc = new("sqacc", [P, T])
        rstd = new("rstd", [P, T])
        ident = new("ident", [P, P])
        ones = new("ones", [P, P])
        identb = new("identb", [P, P], BF16)
        maskneg = new("maskneg", [P, P], BF16)
        vrows = new("vrows", [NVEC, P])
        gcol = new("gcol", [P, NVEC])
        epsc = new("epsc", [P, 1])
        biasrow = new("biasrow", [1, P])
        biasbc = new("biasbc", [P, SH])
        nbiasbc = new("nbiasbc", [P, SH])
        biascol = new("biascol", [P, 1])
        nbiascol = new("nbiascol", [P, 1])
        ptab = new("ptab", [1, NPAGES], I32)
        off_phase = top[0]
        qT = new("qT", [P, GH, T])
        kT = new("kT", [P, GH, T])
        gkT = new("gkT", [P, GH, T])
        gT = new("gT", [P, KT, T])
        vtok = new("vtok", [P, TB, D])
        vs = new("vs", [NS, D])
        pT_hi, pT_lo = new("pT_hi", [P, 2, T], F32R), new("pT_lo", [P, 2, T], F32R)
        k_s = new("k_s", [NS, GH * HK])
        chmask = new("chmask", [P, NP_TOK])
        attmask = new("attmask", [P, P])
        dec = new("dec", [P, GH, NCH])
        w2 = new("w2", [RANK, GH * HK])
        ps0 = new("ps0", [NS, PLE])
        kb8 = size([P, GH, NP_TOK])
        kdtok = at("kdtok", [P, GH, TB, P], F32, offB)
        attT = at("attT", [P, GH, NP_TOK], F32, offB + kb8)
        gE = at("gE", [P, GH, NP_TOK], F32, offB + 2 * kb8)
        gD = at("gD", [P, GH, NP_TOK], F32, offB + 3 * kb8)
        states = at("states", [P, 2, NCH, HV], F32, offB + 2 * kb8)
        s0 = at("s0", [P, NS * GH, HV], F32, offA)
        up0T = at("up0T", [P, KT, T], F32, off_phase)
        end_a, top[0] = top[0], off_phase
        q1T = new("q1T", [P, KT, T])
        K1T = new("K1T", [P, KT, T])
        g1T = new("g1T", [P, KT, T])
        V1 = new("V1", [P, TB, D])
        qb = new("qb", [P, 2, D])
        sel = new("sel", [NS, NS, P])
        up1T = at("up1T", [P, KT, T], F32, off_phase)
        o1 = off_phase + size([P, KT, T])
        pT1_hi = at("pT1_hi", [P, 2, T], F32R, o1)
        pT1_lo = at("pT1_lo", [P, 2, T], F32R, o1 + size([P, 2, T]))
        pin1 = at("pin1", [P, TB, PLE], F32, o1 + 2 * size([P, 2, T]))
        ps1 = at("ps1", [NS, PLE], F32, o1 + 2 * size([P, 2, T]) + size([P, TB, PLE]))
        ystage = at("ystage", [P, TB, D], F32, o1 + size([P, KT, T]))
        ysrow = at("ysrow", [NS, D], F32, o1)
        ring = at("ring", [P, RING, D], F32, offA)
        zall = at("zall", [P, NPG, P], F32, offA + RING * D * 4)
        ssig = at("ssig", [P, PAST], F32, offB)
        scum = at("scum", [P, PAST + 1], F32, offB + PAST * 4)
        pz = size([P, NZ + 4])
        psig = [at(f"psig{i}", [P, NZ], F32, offB + i * pz) for i in range(2)]
        pcum = [at(f"pcum{i}", [P, NZ + 4], F32, offB + (2 + i) * pz) for i in range(2)]
        pat = at("pat", [P, NZ], F32, offB + 4 * pz)

        pp = [ctx.enter_context(nc.psum_tensor(f"pp{i}", [P, 2, 512], F32)) for i in range(4)]
        bank = [pp[i // 2][:, i % 2, :] for i in range(8)]

        def chunk_bank(c):
            return bank[6 + c % 2][:, (c // 2 % 2) * HV:(c // 2 % 2 + 1) * HV]

        sems = {}

        def S(name):
            if name not in sems:
                sems[name] = ctx.enter_context(nc.semaphore(name))
            return sems[name]

        block = ctx.enter_context(nc.Block())

        def weight_pair_source(p):
            name = phase_of(2 * p)
            o = (2 * p - PHASES[name][0]) * P
            w, c0 = {"q": (gla_w_in[0], 0), "k": (gla_w_in[0], 512), "v": (gla_w_in[0], 1024),
                     "g": (gla_w_in[0], 2048), "wo0": (gla_w_out[0], 0), "ple0": (w_ple_gate[0], 0),
                     "q1": (sb_w_in[0], 0), "g1": (sb_w_in[0], D), "K": (w_kv, 0), "V": (w_kv, D),
                     "wo1": (sb_w_out[0], 0), "ple1": (w_ple_gate[1], 0)}[name]
            return w.rearrange("(k p) n -> p k n", p=P)[:, :, c0 + o:c0 + o + 2 * P]

        def raw_pair(p):
            name = phase_of(2 * p)
            return w_raw[:, p % 2, :].rearrange("p (k n) -> p k n", k=2 if name[:2] == "up" else KT)

        def split_views(j):
            k = 2 if phase_of(j)[:2] == "up" else KT
            n = 1024 // k
            return (raw_pair(j // 2)[:, :, n * (j % 2):n * (j % 2) + n],
                    w_hi[j % 2][:].rearrange("p (k n) -> p k n", k=k),
                    w_lo[j % 2][:].rearrange("p (k n) -> p k n", k=k))

        def x_parts(n):
            hi, lo = (xa_hi, xa_lo) if "ABABBA"[n // KT] == "A" else (xb_hi, xb_lo)
            return hi[:, n % KT, :], lo[:, n % KT, :]

        def last_tile(name):
            j0, n, _ = PHASES[name]
            return tiles_through(j0 + n - 1)

        @block.sync
        def _(sp):
            for r0, n, v in ((0, 16, g_pre), (16, 16, g_ple), (32, 8, g_kv), (GFINAL, 8, g_final),
                             (GOUT, 2, gla_g_out), (BGK, 4, gla_b_gk)):
                flat = v if len(v.shape) == 1 else v.rearrange("a b -> (a b)")
                sp.dma_start(vrows[r0:r0 + n, :], flat.rearrange("(r c) -> r c", c=P)).then_inc(S("vec_in"), 16)
            sp.dma_start(vtok[:, :, :], x_prompt[0].rearrange("(b p) d -> p b d", p=P)).then_inc(S("x_in"), 16)
            sp.dma_start(vs[:, :], x_sample[:, 0, :]).then_inc(S("x_in"), 16)
            sp.wait_ge(S("raw_zero"), 1)
            sp.dma_start(raw_pair(0)[:, :, 0:RANK],
                         gla_w_in[0].rearrange("(k p) n -> p k n", p=P)[:, :, 3072:3072 + RANK]).then_inc(S("w_in0"), 16)
            sp.dma_start(gT[:, 0:TB, 0:PLE], p_prompt[0, 0].rearrange("(b p) d -> p b d", p=P)).then_inc(S("p_in"), 16)
            sp.dma_start(ps0[:, :], p_sample[0, :, 0, :]).then_inc(S("p_in"), 16)
            sp.dma_start(w2[:, :], gla_w_gk2[0]).then_inc(S("w2_in"), 16)
            sp.dma_start(ptab[0:1, :], page_table.rearrange("b n -> (b n)").rearrange("(o n) -> o n", o=1)).then_inc(S("ptab_in"), 16)
            sp.dma_start(biasrow[0:1, 0:SH], sb_bias).then_inc(S("bias_in"), 16)

            def load_pair(p):
                if p >= 2:
                    sp.wait_ge(S("w_split"), 2 * (p - 1))
                src = (w_ple_up[int(phase_of(2 * p)[2])].rearrange("(k p) n -> p k n", p=P)
                       if phase_of(2 * p)[:2] == "up" else weight_pair_source(p))
                sp.dma_start(raw_pair(p), src).then_inc(S(f"w_in{p % 2}"), 16)

            def load_page(n):
                idx = sp.value_load(ptab[0:1, n % NPAGES:n % NPAGES + 1], min_val=0, max_val=cache_k.shape[0] - 1)
                src = cache_k if n < NPAGES else cache_v
                if n >= RING:
                    m = n - RING
                    if m < NPAGES:
                        sp.wait_ge(S("k_used"), m + 1)
                    else:
                        sp.wait_ge(S("v_used"), m - NPAGES + 1)
                sp.dma_start(ring[:, n % RING, :],
                             src[bass.ds(idx, 1)].rearrange("o t h d -> (o t) (h d)")).then_inc(S(f"page_in{n % RING}"), 16)

            q1 = PHASES["q1"][0] // 2
            for p in range(1, q1):
                load_pair(p)
                if 2 * p == PHASES["up0"][0] + 2:
                    sp.wait_ge(S("mm"), last_tile("g"))
                    sp.dma_start(s0[:, :, :], state_gla[0].rearrange("b h k v -> k (b h) v")).then_inc(S("s0_in"), 16)
            g1, up1 = PHASES["g1"][0] // 2, PHASES["up1"][0] // 2
            for p in range(q1, g1 + 2):
                load_pair(p)
            sp.wait_ge(S("ptab_in"), 16)
            sp.wait_ge(S("mm"), last_tile("ple0"))
            for n in range(RING):
                load_page(n)
            n = RING
            for p in range(g1, up1):
                load_pair(p + 2)
                while n < min(NPAGES, RING + 2 * K_PER_JOB * (p + 1 - g1)):
                    load_page(n)
                    n += 1
            while n < 2 * NPAGES:
                load_page(n)
                n += 1
            sp.wait_ge(S("z_p"), SH)
            sp.dma_start(pin1[:, :, :], p_prompt[1, 0].rearrange("(b p) d -> p b d", p=P)).then_inc(S("p1_in"), 16)
            sp.dma_start(ps1[:, :], p_sample[1, :, 0, :]).then_inc(S("p1_in"), 16)
            for p in range(PHASES["up1"][0] // 2 + 2, NJOBS // 2):
                load_pair(p)
            for k in range(KT):
                sp.wait_ge(S("y_out"), k + 1)
                sp.dma_start(y_prompt[0].rearrange("(b p) d -> p b d", p=P)[:, :, k * P:(k + 1) * P],
                             ystage[:, :, k * P:(k + 1) * P]).then_inc(S("results"), 16)
            sp.dma_start(y_sample[:, 0, :], ysrow[:, :]).then_inc(S("results"), 16)
            sp.wait_ge(S("results"), 16 * (KT + 1))
            for e in range(2):
                sp.wait_ge(S(f"st_out{e}"), 16 * GH // 2)
            sp.wait_ge(S("ss_out"), 16)
            sp.wait_ge(S("kv_ss"), 16 * 4)
            for e in range(4):
                sp.wait_ge(S(f"k_st{e}"), 16 * KT // 4)
            sp.wait_ge(S("v_st"), 16)

        @block.gpsimd
        def _(pool):
            own = Steps(pool, S("pool_steps"))
            nc.gpsimd.memset(w_raw[:, 0, :], 0.0).then_inc(S("raw_zero"), 1)
            nc.gpsimd.memset(attmask[:], 1.0)
            nc.gpsimd.memset(chmask[:], 1.0)
            nc.gpsimd.memset(maskneg[:], NEG)
            own.then(nc.gpsimd.memset(ident[:], 0.0))
            nc.gpsimd.affine_select(out=ident[:], in_=ident[:], compare_op=ALU.not_equal, fill=1.0, base=0,
                                    pattern=[[-1, P]], channel_multiplier=1).then_inc(S("ident"), 1)
            pool.wait_ge(S("ident"), 1)
            nc.gpsimd.tensor_copy(identb[:], ident[:])
            nc.gpsimd.affine_select(out=maskneg[:], in_=maskneg[:], compare_op=ALU.is_ge, fill=0.0, base=0,
                                    pattern=[[1, P]], channel_multiplier=-1)
            nc.gpsimd.memset(chmask[:, 0:NP_TOK:CH], 0.0)
            own.then(nc.gpsimd.memset(attmask[0:CH, CH:P], 0.0))
            nc.gpsimd.affine_select(out=attmask[:], in_=attmask[:], compare_op=ALU.is_ge, fill=0.0, base=0,
                                    pattern=[[1, P]], channel_multiplier=-1)
            nc.gpsimd.memset(attT[:], 0.0)
            nc.gpsimd.memset(ones[:], 1.0)
            nc.gpsimd.memset(epsc[:], EPS).then_inc(S("consts"), 1)

            def scale_pair(p):
                if p >= NJOBS // 2 or GAIN[phase_of(2 * p)] is None:
                    return
                g0 = GAIN[phase_of(2 * p)]
                pool.wait_ge(S(f"w_in{p % 2}"), 16 * (p // 2 + 1))
                if p == 0:
                    pool.wait_ge(S("gcol"), 1)
                v = raw_pair(p)
                if g0 == GOUT:
                    v = v.rearrange("p (a c) n -> p a c n", c=2)
                    g = gcol[:, g0:g0 + 2].unsqueeze(1).unsqueeze(3).to_broadcast([P, GH, 2, 2 * P])
                else:
                    g = gcol[:, g0:g0 + KT].unsqueeze(2).to_broadcast([P, KT, 2 * P])
                nc.gpsimd.tensor_tensor(v, v, g, ALU.mult).then_inc(S("w_scaled"), 1)

            def sum_squares(n):
                pool.wait_ge(S("sq"), n + 1)
                if n % KT == 0:
                    if n:
                        pool.wait_ge(S("ss_mm"), n // KT)
                    if n == 3 * KT:
                        pool.wait_ge(S("kv_ss"), 64)
                    nc.gpsimd.tensor_copy(sqacc[:], work[:, n % 2, :]).then_inc(S("sq_added"), 1)
                else:
                    pool.wait_ge(S("sq_added"), n)
                    nc.gpsimd.tensor_tensor(sqacc[:], sqacc[:], work[:, n % 2, :], ALU.add).then_inc(S("sq_added"), 1)

            def multiply_page(n):
                pool.wait_ge(S("qb_in"), n // NPG + 1)
                pool.wait_ge(S(f"page_in{n % RING}"), 16 * (n // RING + 1))
                nc.gpsimd.tensor_tensor(ring[:, n % RING, :], ring[:, n % RING, :], qb[:, (n // NPG) % 2, :],
                                        ALU.mult).then_inc(S("k_mul_pool"), 1)

            scale_pair(0)
            scale_pair(1)
            for n in range(KT):
                sum_squares(n)
            for p in range(2, PHASES["wo0"][0] // 2 + 2):
                scale_pair(p)
            for i, (name, h) in enumerate((("wo0", 1), ("ple0", 2))):
                for u in range(8):
                    sum_squares(h * KT + u)
                    if u % 2 == 0:
                        scale_pair(PHASES[name][0] // 2 + 2 + u // 2)
            for u in range(4):
                scale_pair(PHASES["q1"][0] // 2 + 2 + u)
            pool.wait_ge(S("evac"), last_tile("ple0") + 1)
            own.then(nc.gpsimd.memset(sel[:], 0.0))
            nc.gpsimd.affine_select(out=sel[:], in_=sel[:], compare_op=ALU.not_equal, fill=1.0, base=0,
                                    pattern=[[-1, NS], [0, P]], channel_multiplier=1).then_inc(S("sel"), 1)
            n = 0
            for i in range(24):
                for _ in range(K_PER_JOB):
                    if n % 5 in POOL_SHARE:
                        multiply_page(n)
                    n += 1
                if i % 2 == 0:
                    scale_pair(PHASES["g1"][0] // 2 + 2 + i // 2)
            while n < NPAGES:
                if n % 5 in POOL_SHARE:
                    multiply_page(n)
                n += 1
            for i, name in enumerate(("wo1", "ple1")):
                for u in range(8):
                    sum_squares((3 + i) * KT + u)
                    if u % 2 == 0:
                        scale_pair(PHASES[name][0] // 2 + 2 + u // 2)

        @block.scalar
        def _(act):
            own = Steps(act, S("act_steps"))
            act.wait_ge(S("consts"), 1)
            act.wait_ge(S("gcol_t"), 1)
            nc.scalar.copy(gcol[:], bank[7][:, 0:NVEC]).then_inc(S("gcol"), 1)

            def split_hi(j):
                if j >= NJOBS:
                    return
                p = j // 2
                if GAIN[phase_of(j)] is None:
                    act.wait_ge(S(f"w_in{p % 2}"), 16 * (p // 2 + 1))
                else:
                    act.wait_ge(S("w_scaled"), gains_through(p))
                if j >= 2:
                    act.wait_ge(S("mm"), tiles_through(j - 2))
                if j == 3:
                    act.wait_ge(S("w_split"), 2)
                raw, hi, _ = split_views(j)
                nc.scalar.copy(hi, raw).then_inc(S("w_hi"), 1)

            def x_hi(n, src):
                nc.scalar.copy(x_parts(n)[0], src).then_inc(S("x_hi"), 1)

            def square(n, src):
                if n >= 2:
                    act.wait_ge(S("sq_added"), n - 1)
                nc.scalar.activation(work[:, n % 2, :], src, ACT.Square).then_inc(S("sq"), 1)

            def rms(i):
                act.wait_ge(S("ss_mm"), i + 1)
                nc.scalar.activation(rstd[:].rearrange("p (t n) -> p t n", t=2), pp[3][:, :, 0:H2], ACT.Sqrt,
                                     bias=epsc[:], scale=1.0 / D).then_inc(S("r_sqrt"), 1)

            def sigmoid_tile(n, src, dst):
                nc.scalar.activation(dst, src, ACT.Sigmoid).then_inc(S("sigm"), 1)

            for k in range(KT):
                act.wait_ge(S("xt"), k + 1)
                nc.scalar.copy(hT[:, k, 0:NP_TOK], bank[4 + k % 2])
                own.did(nc.scalar.copy(hT[:, k, NP_TOK:T], bank[6 + k % 2][:, 64:64 + NS]))
                own.wait()
                x_hi(k, hT[:, k, :])
                square(k, hT[:, k, :])
            split_hi(0)
            for c in range(2):
                act.wait_ge(S("pt"), c + 1)
                nc.scalar.copy(pT_hi[:, c, 0:NP_TOK], bank[4 + c])
                nc.scalar.copy(pT_hi[:, c, NP_TOK:T], bank[6 + c][:, 64:64 + NS]).then_inc(S("pt_hi"), 1)
            split_hi(1)
            rms(0)
            for u in range(4):
                split_hi(PHASES["q"][0] + u)
            split_hi(PHASES["k"][0])
            for h in range(GH):
                act.wait_ge(S("gk_out"), h + 1)
                own.then(nc.scalar.activation(gE[:, h, :], gkT[:, h, 0:NP_TOK], ACT.Abs))
                own.then(nc.scalar.activation(gE[:, h, :], gE[:, h, :], ACT.Exp, scale=-1.0))
                nc.scalar.activation(gE[:, h, :], gE[:, h, :], ACT.Ln, bias=1.0)
                own.then(nc.scalar.activation(gD[:, h, 0:NS], gkT[:, h, NP_TOK:T], ACT.Abs))
                own.then(nc.scalar.activation(gD[:, h, 0:NS], gD[:, h, 0:NS], ACT.Exp, scale=-1.0))
                nc.scalar.activation(gD[:, h, 0:NS], gD[:, h, 0:NS], ACT.Ln, bias=1.0).then_inc(S("gk_ln"), 1)
                split_hi(PHASES["k"][0] + h + 1)

            def v_rows(u):
                act.wait_ge(S("v_t"), u + 1)
                nc.scalar.copy(vtok[:, :, u * P:(u + 1) * P], bank[4].rearrange("p (b n) -> p b n", b=TB))
                nc.scalar.copy(vs[:, u * P:(u + 1) * P], bank[5][0:NS, 0:P]).then_inc(S("v_out"), 1)

            for u in range(8):
                split_hi(PHASES["v"][0] + u + 1)
                if u == 0:
                    act.wait_ge(S("ks_t"), 1)
                    nc.scalar.copy(k_s[:], bank[4][0:NS, :]).then_inc(S("ks_out"), 1)
                else:
                    v_rows(u - 1)
                if 1 <= u <= 4:
                    h = u - 1
                    act.wait_ge(S("gk_d"), h + 1)
                    nc.scalar.activation(dec[:, h, :], gkT[:, h, CH - 1:NP_TOK:CH], ACT.Exp, scale=1 / GATE_NORM)
                    nc.scalar.activation(gE[:, h, :], gkT[:, h, 0:NP_TOK], ACT.Exp, scale=1 / GATE_NORM)
                    own.did(nc.scalar.activation(gkT[:, h, NP_TOK:T], gkT[:, h, NP_TOK:T], ACT.Exp, scale=1 / GATE_NORM))
                    nc.scalar.activation(gD[:, h, :], gD[:, h, :], ACT.Exp, scale=1 / GATE_NORM)
                    own.wait()
                    nc.scalar.activation(gkT[:, h, 0:NP_TOK], gkT[:, h, 0:NP_TOK], ACT.Exp,
                                         scale=-1 / GATE_NORM).then_inc(S("gk_e"), 1)

            def o_copies(h):
                act.wait_ge(S("o_mm"), h + 1)
                if h:
                    act.wait_ge(S("oss_mm"), h)
                nc.scalar.copy(qT[:, h, 0:NP_TOK], bank[6])
                nc.scalar.copy(kT[:, h, 0:NP_TOK], bank[7])
                nc.scalar.activation(work[:, 0, 0:NP_TOK], bank[6], ACT.Square)
                nc.scalar.activation(work[:, 1, 0:NP_TOK], bank[7], ACT.Square).then_inc(S("o_out"), 1)
                act.dma_start(st_prompt[0, 0, h], states[:, h % 2, NCH - 1, :]).then_inc(S(f"st_out{h % 2}"), 16)

            def o_rms(h):
                act.wait_ge(S("oss_mm"), h + 1)
                nc.scalar.activation(gkT[:, h, 0:NP_TOK], bank[4], ACT.Sqrt, bias=epsc[:],
                                     scale=1.0 / HV).then_inc(S("o_sqrt"), 1)

            for u in range(8):
                h = u // 2
                split_hi(PHASES["g"][0] + u + 1)
                if u == 0:
                    v_rows(7)
                if u >= 2:
                    act.wait_ge(S("silu"), u - 1)
                act.wait_ge(S("evac"), PHASES["g"][2] + u + 1)
                sigmoid_tile(u, gT[:, u, :], work[:, 2 + u % 2, :])
                if u % 2 == 0:
                    if h:
                        o_copies(h - 1)
                    act.wait_ge(S("kd_t"), h + 1)
                    nc.scalar.copy(kdtok[:, h].rearrange("p b n -> p (b n)"), bank[4]).then_inc(S("kd_out"), 1)
                elif h:
                    o_rms(h - 1)
            o_copies(GH - 1)
            split_hi(PHASES["up0"][0] + 1)
            o_rms(GH - 1)
            act.wait_ge(S("s_new"), NS * GH)
            act.dma_start(st_sample[0].rearrange("b h k v -> k (b h) v"), s0[:, :, :]).then_inc(S("ss_out"), 16)
            act.wait_ge(S("so_mm"), 1)
            nc.scalar.activation(work[:, 2, 0:64], bank[4][:, 0:64], ACT.Square).then_inc(S("sosq"), 1)
            act.wait_ge(S("soss_mm"), 1)
            nc.scalar.activation(work[:, 3, 0:32], bank[5][:, 0:32], ACT.Sqrt, bias=epsc[:],
                                 scale=1.0 / HV).then_inc(S("so_sqrt"), 1)
            act.wait_ge(S("so_used"), 1)
            split_hi(PHASES["up0"][0] + 2)
            for e in range(2):
                act.wait_ge(S(f"st_out{e}"), 16 * GH // 2)
            for i in range(KT):
                x_hi(KT + i, gT[:, i, :])
            for u in range(8):
                j = PHASES["wo0"][0] + u
                split_hi(j + 1)
                if u == 0:
                    act.wait_ge(S("ss_out"), 16)
                act.wait_ge(S("evac"), tiles_through(j))
                x_hi(2 * KT + u, hT[:, u, :])
                square(KT + u, hT[:, u, :])
            for u in range(8):
                j = PHASES["ple0"][0] + u
                split_hi(j + 1)
                if u == 0:
                    rms(1)
                act.wait_ge(S("evac"), tiles_through(j))
                sigmoid_tile(8 + u, work[:, 2 + u % 2, :], work[:, 2 + u % 2, :])
                act.wait_ge(S("h_new"), u + 1)
                x_hi(3 * KT + u, hT[:, u, :])
                square(2 * KT + u, hT[:, u, :])
            for u in range(8):
                j = PHASES["q1"][0] + u
                split_hi(j + 1)
                if u == 0:
                    rms(2)
            act.wait_ge(S("qs_t"), 1)
            qs = work[0:NS, 0:2, 0:512]
            nc.scalar.copy(qs, pp[2][0:NS, :, :]).then_inc(S("qs_out"), 1)

            def query_out(b):
                act.wait_ge(S("qb_mm"), b + 1)
                if b >= 2:
                    act.wait_ge(S("k_used"), (b - 1) * NPG)
                nc.scalar.copy(qb[:, b % 2, :].rearrange("p (t n) -> p t n", t=2), pp[3][:, :, :]).then_inc(S("qb_in"), 1)

            act.wait_ge(S("bias_mm"), 1)
            nc.scalar.copy(biasbc[:], bank[4][:, 0:SH])
            nc.scalar.activation(nbiasbc[:], bank[4][:, 0:SH], ACT.Copy, scale=-1.0)
            nc.scalar.copy(biascol[:], bank[5][:, 0:1])
            nc.scalar.activation(nbiascol[:], bank[5][:, 0:1], ACT.Copy, scale=-1.0).then_inc(S("bias_out"), 1)

            query_out(0)
            query_out(1)
            asked = 2

            def kv_tile(t):
                u = t % 8
                dst = V1[:, :, u * P:(u + 1) * P]
                if t >= 8:
                    act.wait_ge(S(f"k_st{u % 4}"), 32)
                act.wait_ge(S("kv_t"), t + 1)
                nc.scalar.copy(dst, bank[4].rearrange("p (b n) -> p b n", b=TB))
                if t % 4 == 0 and t:
                    act.wait_ge(S("kv_ss"), 16 * (t // 4))
                nc.scalar.copy(sqacc[0:NS, (t % 4) * P:(t % 4 + 1) * P], bank[5][0:NS, 0:P]).then_inc(S("kv_out"), 1)
                act.wait_ge(S("kv_out"), t + 1)
                if t < 8:
                    act.dma_start(k_prompt[0].rearrange("(b p) h d -> p b (h d)", p=P)[:, :, u * P:(u + 1) * P],
                                  dst).then_inc(S(f"k_st{u % 4}"), 16)
                if t % 4 == 3:
                    out = (k_sample if t < 8 else v_sample)[:, 0].rearrange("b h d -> b (h d)")
                    c0 = (u - 3) * P
                    act.dma_start(out[:, c0:c0 + 512], sqacc[0:NS, 0:512]).then_inc(S("kv_ss"), 16)
                if t == 15:
                    act.dma_start(v_prompt[0].rearrange("(b p) h d -> p b (h d)", p=P), V1[:, :, :]).then_inc(S("v_st"), 16)

            for i in range(24):
                j = PHASES["g1"][0] + i
                split_hi(j + 1)
                if i < 8:
                    act.wait_ge(S("evac"), tiles_through(j))
                    if i >= 2:
                        act.wait_ge(S("silu"), 8 + i - 1)
                    sigmoid_tile(16 + i, g1T[:, i, :], work[:, 2 + i % 2, :])
                while asked < NS and asked <= (i * K_PER_JOB) // NPG + 1 and i >= 1:
                    query_out(asked)
                    asked += 1
                if i >= KV_LAG + 8:
                    kv_tile(i - KV_LAG - 8)
            while asked < NS:
                query_out(asked)
                asked += 1
            for t in range(16 - KV_LAG, 16):
                kv_tile(t)
            split_hi(PHASES["up1"][0] + 1)

            act.wait_ge(S("z_t"), 4)
            for g in range(4):
                c = slice(g * 512, (g + 1) * 512)
                nc.scalar.activation(scum[:, c], bank[g], ACT.Sigmoid, bias=nbiascol[:], scale=-HD ** -0.5)
                last = nc.scalar.activation(ssig[:, c], bank[g], ACT.Sigmoid, bias=biascol[:], scale=HD ** -0.5)
            last.then_inc(S("s_sig"), 1)
            for g in range(4):
                act.wait_ge(S("a_t"), g + 1)
                last = nc.scalar.copy(zall[:, 4 * g:4 * g + 4, :].rearrange("p j n -> p (j n)"), bank[g])
                last.then_inc(S("a_out"), 1)

            def head_sigmoids(h):
                act.wait_ge(S("z_p"), h + 1)
                if h >= 2:
                    act.wait_ge(S("at_t"), h - 1)
                for q in (0, 2, 1, 3):
                    bk, c0 = ZB[q]
                    n = (q + 1) * P
                    nc.scalar.activation(pcum[h % 2][:, SEG[q]:SEG[q] + n], bank[bk][:, c0:c0 + n], ACT.Sigmoid,
                                         bias=nbiasbc[:, h:h + 1], scale=-HD ** -0.5)
                for bk, c0, n in ((0, 0, 512), (1, 512, 256), (2, 768, 512)):
                    last = nc.scalar.activation(psig[h % 2][:, c0:c0 + n], bank[bk][:, 0:n], ACT.Sigmoid,
                                                bias=biasbc[:, h:h + 1], scale=HD ** -0.5)
                last.then_inc(S("sig_p"), 1)

            def head_weights(h):
                act.wait_ge(S("at_t"), h + 1)
                if h:
                    act.wait_ge(S("o_p"), h)
                for bk, c0, n in ((3, 0, 512), (4, 512, 384), (5, 896, 384)):
                    last = nc.scalar.copy(pat[:, c0:c0 + n], bank[bk][:, 0:n])
                last.then_inc(S("at_out"), 1)

            head_sigmoids(0)
            for h in range(SH):
                if h + 1 < SH:
                    head_sigmoids(h + 1)
                head_weights(h)
            for c in range(2):
                act.wait_ge(S("pt"), 3 + c)
                nc.scalar.copy(pT1_hi[:, c, 0:NP_TOK], bank[4 + c])
                nc.scalar.copy(pT1_hi[:, c, NP_TOK:T], bank[(3, 6)[c]][:, 0:NS]).then_inc(S("pt_hi"), 1)
            split_hi(PHASES["wo1"][0])
            act.wait_ge(S("so1_used"), 2)
            for i in range(KT):
                x_hi(4 * KT + i, g1T[:, i, :])
            for u in range(8):
                j = PHASES["wo1"][0] + u
                split_hi(j + 1)
                act.wait_ge(S("evac"), tiles_through(j))
                x_hi(5 * KT + u, hT[:, u, :])
                square(3 * KT + u, hT[:, u, :])
            for u in range(8):
                j = PHASES["ple1"][0] + u
                split_hi(j + 1)
                if u == 0:
                    rms(3)
                act.wait_ge(S("evac"), tiles_through(j))
                sigmoid_tile(24 + u, work[:, 2 + u % 2, :], work[:, 2 + u % 2, :])
                act.wait_ge(S("h_new"), 8 + u + 1)
                square(4 * KT + u, hT[:, u, :])
            rms(4)
            for k in range(KT):
                act.wait_ge(S("yt_t"), k + 1)
                nc.scalar.copy(ystage[:, :, k * P:(k + 1) * P], bank[4 + k % 2].rearrange("p (b n) -> p b n", b=TB))
                nc.scalar.copy(ysrow[:, k * P:(k + 1) * P], bank[6 + k % 2][0:NS, 0:P]).then_inc(S("y_out"), 1)

        @block.vector
        def _(dve):
            own = Steps(dve, S("dve_steps"))

            def split_lo(j):
                if j >= NJOBS:
                    return
                dve.wait_ge(S("w_hi"), j + 1)
                raw, hi, lo = split_views(j)
                nc.vector.tensor_tensor(lo, raw, hi.bitcast(F32), ALU.subtract).then_inc(S("w_split"), 1)

            def x_lo(n, src):
                dve.wait_ge(S("x_hi"), n + 1)
                hi, lo = x_parts(n)
                nc.vector.tensor_tensor(lo, src, hi.bitcast(F32), ALU.subtract).then_inc(S("x_ready"), 1)

            def halves(ap):
                return ap.rearrange("p (t n) -> p t n", t=2)

            R2 = halves(rstd[:])

            def product_of(j):
                m = tiles_through(j) - 1
                dve.wait_ge(S("mm"), m + 1)
                return pp[m % 2][:, :, 0:H2]

            def normed(j, dst):
                nc.vector.tensor_tensor(halves(dst), product_of(j), R2, ALU.mult).then_inc(S("evac"), 1)

            def recip(i):
                dve.wait_ge(S("r_sqrt"), i + 1)
                own.then(nc.vector.reciprocal(rstd[:], rstd[:]))

            def embed_lo(hi_t, lo_t, c, pbank, sbank):
                nc.vector.tensor_tensor(lo_t[:, c, 0:NP_TOK], pbank, hi_t[:, c, 0:NP_TOK].bitcast(F32), ALU.subtract)
                nc.vector.tensor_tensor(lo_t[:, c, NP_TOK:T], sbank, hi_t[:, c, NP_TOK:T].bitcast(F32),
                                        ALU.subtract).then_inc(S("p_ready"), 1)

            for k in range(KT):
                x_lo(k, hT[:, k, :])
            split_lo(0)
            for c in range(2):
                dve.wait_ge(S("pt_hi"), c + 1)
                embed_lo(pT_hi, pT_lo, c, bank[4 + c], bank[6 + c][:, 64:64 + NS])
            split_lo(1)
            recip(0)
            split_lo(2)
            nc.vector.tensor_tensor(halves(sqacc[0:RANK, :]), product_of(0)[0:RANK], R2[0:RANK],
                                    ALU.mult).then_inc(S("evac"), 1)

            def decay_logits(h):
                dve.wait_ge(S("gk_mm"), h + 1)
                nc.vector.tensor_scalar(halves(gkT[:, h, :]), pp[2 + h % 2][:, :, 0:H2], gcol[:, BGK + h:BGK + h + 1],
                                        None, ALU.add).then_inc(S("gk_out"), 1)

            for h in range(GH):
                j = PHASES["q"][0] + h
                split_lo(j + 1)
                nc.vector.scalar_tensor_tensor(halves(qT[:, h, :]), product_of(j), HK ** -0.5, R2,
                                               ALU.mult, ALU.mult).then_inc(S("evac"), 1)
                if h:
                    decay_logits(h - 1)
            decay_logits(GH - 1)
            for h in range(GH):
                j = PHASES["k"][0] + h
                split_lo(j + 1)
                normed(j, kT[:, h, :])
            for u in range(8):
                j = PHASES["v"][0] + u
                split_lo(j + 1)
                if u >= 2:
                    dve.wait_ge(S("v_t"), u - 1)
                normed(j, work[:, 2 + u % 2, :])
                if u < GH:
                    h = u
                    dve.wait_ge(S("gk_ln"), h + 1)
                    nc.vector.scalar_tensor_tensor(gkT[:, h, NP_TOK:T], gkT[:, h, NP_TOK:T], 0.0, gD[:, h, 0:NS],
                                                   ALU.min, ALU.subtract)
                    own.then(nc.vector.scalar_tensor_tensor(gkT[:, h, 0:NP_TOK], gkT[:, h, 0:NP_TOK], 0.0, gE[:, h, :],
                                                            ALU.min, ALU.subtract))
                    own.then(nc.vector.tensor_tensor_scan(gkT[:, h, 0:NP_TOK], chmask[:], gkT[:, h, 0:NP_TOK], 0.0,
                                                          ALU.mult, ALU.add))
                    chunks = gkT[:, h, 0:NP_TOK].rearrange("p (c n) -> p c n", n=CH)
                    nc.vector.tensor_tensor(gD[:, h, :].rearrange("p (c n) -> p c n", n=CH),
                                            chunks[:, :, CH - 1:CH].to_broadcast([P, NCH, CH]), chunks,
                                            ALU.subtract).then_inc(S("gk_d"), 1)
                else:
                    h = u - GH
                    dve.wait_ge(S("gk_e"), h + 1)
                    nc.vector.tensor_tensor(qT[:, h, 0:NP_TOK], qT[:, h, 0:NP_TOK], gE[:, h, :], ALU.mult)
                    nc.vector.tensor_tensor(gkT[:, h, 0:NP_TOK], gkT[:, h, 0:NP_TOK], kT[:, h, 0:NP_TOK], ALU.mult)
                    nc.vector.tensor_tensor(kT[:, h, 0:NP_TOK], kT[:, h, 0:NP_TOK], gD[:, h, :],
                                            ALU.mult).then_inc(S("kdec"), 1)

            def state_steps(h):
                if h >= 2:
                    dve.wait_ge(S(f"st_out{h % 2}"), 16)
                    dve.wait_ge(S("o_mm"), h - 1)
                for c in range(NCH):
                    kv = chunk_bank(c)
                    if c % 4 == 0:
                        dve.wait_ge(S("kv_mm"), h * NCH + c + 4)
                    if c == 0:
                        ins = nc.vector.tensor_copy(states[:, h % 2, 0, :], kv)
                    else:
                        dve.wait_ge(S("st_step"), h * NCH + c)
                        ins = nc.vector.scalar_tensor_tensor(states[:, h % 2, c, :], states[:, h % 2, c - 1, :],
                                                             dec[:, h, c:c + 1], kv, ALU.mult, ALU.add)
                    ins.then_inc(S("st_step"), 1)

            def gate_o(h):
                dve.wait_ge(S("o_sqrt"), h + 1)
                r = gkT[:, h, 0:NP_TOK]
                own.then(nc.vector.reciprocal(r, r))
                nc.vector.tensor_tensor(qT[:, h, 0:NP_TOK], qT[:, h, 0:NP_TOK], r, ALU.mult)
                own.then(nc.vector.tensor_tensor(kT[:, h, 0:NP_TOK], kT[:, h, 0:NP_TOK], r, ALU.mult))
                for vt, o in enumerate((qT, kT)):
                    g = gT[:, 2 * h + vt, 0:NP_TOK]
                    last = nc.vector.tensor_tensor(g, g, o[:, h, 0:NP_TOK], ALU.mult)
                last.then_inc(S("gated"), 1)

            attm = attmask[:].bitcast(I32).unsqueeze(1).to_broadcast([P, TB, P])
            for u in range(8):
                h = u // 2
                j = PHASES["g"][0] + u
                split_lo(j + 1)
                normed(j, gT[:, u, :])
                dve.wait_ge(S("sigm"), u + 1)
                nc.vector.tensor_tensor(gT[:, u, :], gT[:, u, :], work[:, 2 + u % 2, :], ALU.mult).then_inc(S("silu"), 1)
                if u % 2 == 0:
                    dve.wait_ge(S("att_mm"), h + 1)
                    nc.vector.copy_predicated(attT[:, h, :].rearrange("p (b n) -> p b n", b=TB), attm,
                                              bank[5].rearrange("p (b n) -> p b n", b=TB)).then_inc(S("att_out"), 1)
                else:
                    state_steps(h)
                    if h:
                        gate_o(h - 1)

            def up_tiles(j, dst):
                for c in range(4):
                    m = tiles_through(j) - 4 + c
                    dve.wait_ge(S("mm"), m + 1)
                    nc.vector.tensor_copy(halves(dst[:, (j % 2) * 4 + c, :]), pp[m % 2][:, :, 0:H2]).then_inc(S("evac"), 1)

            def key_row(b):
                if b >= 2:
                    dve.wait_ge(S("skv_mm"), (b - 1) * GH)
                nc.vector.tensor_scalar(krow[:, b % 2, :], k_s[:], ident[0:NS, b:b + 1], None,
                                        ALU.mult).then_inc(S("key_row"), 1)

            krow = attT[0:NS, 0:2, :]
            j = PHASES["up0"][0]
            split_lo(j + 1)
            gate_o(GH - 1)
            dve.wait_ge(S("o_mm"), GH)
            key_row(0)
            key_row(1)
            dve.wait_ge(S("s0_in"), 16)
            for b in range(NS):
                if b >= 2:
                    key_row(b)
                for h in range(GH):
                    n = b * GH + h
                    dve.wait_ge(S("skv_mm"), n + 1)
                    nc.vector.scalar_tensor_tensor(s0[:, n, :], s0[:, n, :], gkT[:, h, NP_TOK + b:NP_TOK + b + 1],
                                                   bank[4 + n % 4][:, 0:HV], ALU.mult, ALU.add).then_inc(S("s_new"), 1)
            dve.wait_ge(S("so_sqrt"), 1)
            own.then(nc.vector.reciprocal(work[:, 3, 32:64], work[:, 3, 0:32]))
            so = work[:, 2, 64:128]
            own.then(nc.vector.tensor_tensor(
                so.rearrange("p (h v b) -> p h v b", h=GH, v=2), bank[4][:, 0:64].rearrange("p (h v b) -> p h v b", h=GH, v=2),
                work[:, 3, 32:64].rearrange("p (h b) -> p h b", h=GH).unsqueeze(2).to_broadcast([P, GH, 2, NS]), ALU.mult))
            nc.vector.tensor_tensor(gT[:, :, NP_TOK:T], gT[:, :, NP_TOK:T], so.rearrange("p (i b) -> p i b", b=NS),
                                    ALU.mult).then_inc(S("so_used"), 1)
            up_tiles(j, up0T)
            split_lo(j + 2)
            up_tiles(j + 1, up0T)
            for i in range(KT):
                x_lo(KT + i, gT[:, i, :])

            def add_residual(j, u):
                nc.vector.tensor_tensor(halves(hT[:, u, :]), product_of(j), halves(hT[:, u, :]), ALU.add).then_inc(S("evac"), 1)

            def add_gated(j, u, up, n):
                g = work[:, 2 + u % 2, :]
                normed(j, g)
                dve.wait_ge(S("sigm"), n + 1)
                own.then(nc.vector.tensor_tensor(g, g, up[:, u, :], ALU.mult))
                nc.vector.tensor_tensor(hT[:, u, :], hT[:, u, :], g, ALU.add).then_inc(S("h_new"), 1)

            for u in range(8):
                j = PHASES["wo0"][0] + u
                split_lo(j + 1)
                add_residual(j, u)
                x_lo(2 * KT + u, hT[:, u, :])
            for u in range(8):
                j = PHASES["ple0"][0] + u
                split_lo(j + 1)
                if u == 0:
                    recip(1)
                add_gated(j, u, up0T, 8 + u)
                x_lo(3 * KT + u, hT[:, u, :])
            for u in range(8):
                j = PHASES["q1"][0] + u
                split_lo(j + 1)
                if u == 0:
                    recip(2)
                normed(j, q1T[:, u, :])
            dve.wait_ge(S("bias_in"), 16)
            nc.vector.tensor_copy(biasrow[0:1, SH:P].rearrange("o (b h) -> o b h", h=SH),
                                  biasrow[0:1, 0:SH].unsqueeze(1).to_broadcast([1, NS - 1, SH])).then_inc(S("bias_row"), 1)

            def score_page(n):
                slot = ring[:, n % RING, :]
                if n % 5 in POOL_SHARE:
                    dve.wait_ge(S("k_mul_pool"), pool_pages(n + 1))
                else:
                    dve.wait_ge(S("qb_in"), n // NPG + 1)
                    dve.wait_ge(S(f"page_in{n % RING}"), 16 * (n // RING + 1))
                    own.then(nc.vector.tensor_tensor(slot, slot, qb[:, (n // NPG) % 2, :], ALU.mult))
                b = n // NPG
                nc.vector.tensor_reduce(zall[:, n % NPG, b * SH:(b + 1) * SH], slot.rearrange("p (h d) -> p h d", d=HD),
                                        AX.X, ALU.add).then_inc(S("k_used"), 1)

            n = 0
            for i in range(24):
                u = i % 8
                j = PHASES["g1"][0] + i
                split_lo(j + 1)
                if i < 8:
                    normed(j, g1T[:, u, :])
                    dve.wait_ge(S("sigm"), 16 + u + 1)
                    nc.vector.tensor_tensor(g1T[:, u, :], g1T[:, u, :], work[:, 2 + u % 2, :], ALU.mult).then_inc(S("silu"), 1)
                elif i < 16:
                    normed(j, K1T[:, u, :])
                else:
                    if u >= 2:
                        dve.wait_ge(S("kv_t"), 8 + u - 1)
                    normed(j, work[:, 2 + u % 2, :])
                for _ in range(K_PER_JOB):
                    score_page(n)
                    n += 1
            while n < NPAGES:
                score_page(n)
                n += 1
            split_lo(PHASES["up1"][0] + 1)

            nc.vector.memset(scum[:, PAST:PAST + 1], 1.0)
            dve.wait_ge(S("s_sig"), 1)
            own.then(nc.vector.tensor_tensor_scan(scum[:, PAST - 1::-1], scum[:, PAST - 1::-1],
                                                  ones[:, 0:1].to_broadcast([P, PAST]), 1.0, ALU.mult, ALU.mult))
            nc.vector.tensor_tensor(ssig[:], ssig[:], scum[:, 1:PAST + 1], ALU.mult).then_inc(S("a_s"), 1)
            dve.wait_ge(S("a_t"), 4)
            for i in range(2):
                for q in range(TB):
                    c = SEG[q] + (q + 1) * P
                    own.did(nc.vector.memset(pcum[i][:, c:c + 1], 1.0))

            def head_products(h):
                dve.wait_ge(S("sig_p"), h + 1)
                A, C = psig[h % 2], pcum[h % 2]
                for q in range(TB):
                    n, s = (q + 1) * P, SEG[q]
                    rev = C[:, s + n - 1:s - 1:-1] if s else C[:, n - 1::-1]
                    own.did(nc.vector.tensor_tensor_scan(rev, rev, ones[:, 0:1].to_broadcast([P, n]), 1.0,
                                                         ALU.mult, ALU.mult))
                own.wait()
                for q in range(TB):
                    n, s = (q + 1) * P, SEG[q]
                    a = A[:, PSEG[q]:PSEG[q] + n]
                    last = nc.vector.tensor_tensor(a, a, C[:, s + 1:s + n + 1], ALU.mult)
                last.then_inc(S("a_p"), 1)

            def gate_pair(i):
                dve.wait_ge(S("o_p"), 2 * i + 2)
                nc.vector.tensor_tensor(g1T[:, i, 0:NP_TOK], bank[6], g1T[:, i, 0:NP_TOK], ALU.mult).then_inc(S("u1_out"), 1)

            for h in range(SH):
                head_products(h)
                if h % 2 == 0 and h:
                    gate_pair(h // 2 - 1)
            gate_pair(SH // 2 - 1)
            for c in range(2):
                dve.wait_ge(S("pt_hi"), 3 + c)
                embed_lo(pT1_hi, pT1_lo, c, bank[4 + c], bank[(3, 6)[c]][:, 0:NS])
            j = PHASES["up1"][0]
            up_tiles(j, up1T)
            split_lo(j + 2)
            up_tiles(j + 1, up1T)
            dve.wait_ge(S("v_used"), NPAGES)
            for e in range(2):
                part = slice(e * HD, (e + 1) * HD)
                o = bank[7][part, 0:P].rearrange("p (b i e) -> p i b e", b=NS, e=2)[:, :, :, e]
                nc.vector.tensor_tensor(g1T[part, :, NP_TOK:T], o, g1T[part, :, NP_TOK:T], ALU.mult).then_inc(S("so1_used"), 1)
            for i in range(KT):
                x_lo(4 * KT + i, g1T[:, i, :])
            for u in range(8):
                j = PHASES["wo1"][0] + u
                split_lo(j + 1)
                add_residual(j, u)
                x_lo(5 * KT + u, hT[:, u, :])
            for u in range(8):
                j = PHASES["ple1"][0] + u
                split_lo(j + 1)
                if u == 0:
                    recip(3)
                add_gated(j, u, up1T, 24 + u)
            recip(4)
            for k in range(KT):
                if k >= 2:
                    dve.wait_ge(S("yt_t"), k - 1)
                nc.vector.scalar_tensor_tensor(work[:, 2 + k % 2, :], hT[:, k, :], gcol[:, GFINAL + k:GFINAL + k + 1],
                                               rstd[:], ALU.mult, ALU.mult).then_inc(S("y_t"), 1)

        @block.tensor
        def _(pe):
            pe.wait_ge(S("consts"), 1)
            pe.wait_ge(S("vec_in"), 96)
            nc.tensor.transpose(bank[7][:, 0:NVEC], vrows[:, :], ident[0:NVEC, 0:NVEC]).then_inc(S("gcol_t"), 1)
            pe.wait_ge(S("x_in"), 32)
            pe.wait_ge(S("gcol"), 1)
            for k in range(KT):
                if k >= 2:
                    pe.wait_ge(S("x_hi"), k - 1)
                for b in range(TB):
                    nc.tensor.transpose(bank[4 + k % 2][:, b * P:(b + 1) * P], vtok[:, b, k * P:(k + 1) * P], ident[:])
                nc.tensor.transpose(bank[6 + k % 2][:, 64:64 + NS], vs[:, k * P:(k + 1) * P],
                                    ident[0:NS, 0:NS]).then_inc(S("xt"), 1)
            pe.wait_ge(S("p_in"), 32)
            pe.wait_ge(S("gcol"), 1)
            pe.wait_ge(S("x_hi"), KT)
            for c in range(2):
                for b in range(TB):
                    nc.tensor.transpose(bank[4 + c][:, b * P:(b + 1) * P], gT[:, b, c * P:(c + 1) * P], ident[:])
                nc.tensor.transpose(bank[6 + c][:, 64:64 + NS], ps0[:, c * P:(c + 1) * P],
                                    ident[0:NS, 0:NS]).then_inc(S("pt"), 1)

            def product(j, x0, wait_x=False):
                m = tiles_through(j) - 1
                pe.wait_ge(S("w_split"), j + 1)
                if m >= 2:
                    pe.wait_ge(S("evac"), m - 1)
                _, wh, wl = split_views(j)
                for k in range(KT):
                    if wait_x:
                        pe.wait_ge(S("x_ready"), x0 + k + 1)
                    xh, xl = x_parts(x0 + k)
                    for w, x, first in ((wh, xh, True), (wh, xl, False), (wl, xh, False)):
                        for t in range(2):
                            last = nc.tensor.matmul(pp[m % 2][:, t, 0:H2], w[:, k, :], x[:, t * H2:(t + 1) * H2],
                                                    start=(k == 0 and first), stop=(k == KT - 1 and w is wl))
                last.then_inc(S("mm"), 1)

            def up_product(j, p_hi, p_lo, n):
                pe.wait_ge(S("w_split"), j + 1)
                pe.wait_ge(S("p_ready"), n)
                _, wh, wl = split_views(j)
                for c in range(4):
                    m = tiles_through(j) - 4 + c
                    pe.wait_ge(S("evac"), m - 1)
                    for k in range(2):
                        for w, x, first in ((wh, p_hi, True), (wh, p_lo, False), (wl, p_hi, False)):
                            for t in range(2):
                                last = nc.tensor.matmul(pp[m % 2][:, t, 0:H2], w[:, k, c * P:(c + 1) * P],
                                                        x[:, k, t * H2:(t + 1) * H2],
                                                        start=(k == 0 and first), stop=(k == 1 and w is wl))
                    last.then_inc(S("mm"), 1)

            def square_sum(i):
                pe.wait_ge(S("sq_added"), KT * (i + 1))
                for t in range(2):
                    last = nc.tensor.matmul(pp[3][:, t, 0:H2], ones[:], sqacc[:, t * H2:(t + 1) * H2],
                                            start=True, stop=True)
                last.then_inc(S("ss_mm"), 1)

            def token_major(src, b0, done):
                for b in range(TB):
                    nc.tensor.transpose(bank[b0][:, b * P:(b + 1) * P], src[:, b * P:(b + 1) * P], ident[:])
                nc.tensor.transpose(bank[b0 + 1][0:NS, 0:P], src[:, NP_TOK:T], ident[:]).then_inc(done, 1)

            product(0, 0, wait_x=True)
            pe.wait_ge(S("p_ready"), 2)
            square_sum(0)
            pe.wait_ge(S("w2_in"), 16)
            for h in range(GH):
                product(PHASES["q"][0] + h, 0)
                if h == 0:
                    pe.wait_ge(S("evac"), 1)
                if h >= 2:
                    pe.wait_ge(S("gk_out"), h - 1)
                for t in range(2):
                    last = nc.tensor.matmul(pp[2 + h % 2][:, t, 0:H2], w2[:, h * P:(h + 1) * P],
                                            sqacc[0:RANK, t * H2:(t + 1) * H2], start=True, stop=True)
                last.then_inc(S("gk_mm"), 1)
            for h in range(GH):
                product(PHASES["k"][0] + h, 0)

            def v_tile(u):
                pe.wait_ge(S("evac"), PHASES["v"][2] + u + 1)
                pe.wait_ge(S("v_out"), u) if u else pe.wait_ge(S("ks_out"), 1)
                token_major(work[:, 2 + u % 2, :], 4, S("v_t"))

            for u in range(8):
                product(PHASES["v"][0] + u, 0)
                if u == 0:
                    pe.wait_ge(S("evac"), last_tile("k"))
                    for h in range(GH):
                        last = nc.tensor.transpose(bank[4][0:NS, h * P:(h + 1) * P], kT[:, h, NP_TOK:T], ident[:])
                    last.then_inc(S("ks_t"), 1)
                else:
                    v_tile(u - 1)

            def gla_scores(h):
                pe.wait_ge(S("kdec"), h + 1)
                if h == 0:
                    pe.wait_ge(S("v_out"), 8)
                if h >= 2:
                    pe.wait_ge(S("o_sqrt"), h - 1)
                for b in range(TB):
                    last = nc.tensor.transpose(bank[4][:, b * P:(b + 1) * P], kT[:, h, b * P:(b + 1) * P], ident[:])
                last.then_inc(S("kd_t"), 1)
                if h:
                    pe.wait_ge(S("att_out"), h)
                for b in range(TB):
                    last = nc.tensor.matmul(bank[5][:, b * P:(b + 1) * P], gkT[:, h, b * P:(b + 1) * P],
                                            qT[:, h, b * P:(b + 1) * P], start=True, stop=True)
                last.then_inc(S("att_mm"), 1)

            def gla_states(h):
                pe.wait_ge(S("kd_out"), h + 1)
                if h:
                    pe.wait_ge(S("o_out"), h)
                for c in range(NCH):
                    if c == 4:
                        pe.wait_ge(S("st_step"), h * NCH + 4)
                    r = (c % 2) * CH
                    nc.tensor.matmul(chunk_bank(c), kdtok[r:r + CH, h, c // 2, :], vtok[r:r + CH, c // 2, h * HV:(h + 1) * HV],
                                     start=True, stop=True).then_inc(S("kv_mm"), 1)

            def gla_output(h):
                pe.wait_ge(S("att_out"), h + 1)
                pe.wait_ge(S("st_step"), (h + 1) * NCH)
                for vt in range(2):
                    for b in range(TB):
                        nc.tensor.matmul(bank[6 + vt][:, b * P:(b + 1) * P],
                                         vtok[:, b, h * HV + vt * P:h * HV + (vt + 1) * P],
                                         attT[:, h, b * P:(b + 1) * P], start=(b == 0), stop=False, skip_group_check=True)
                    for c in range(1, NCH):
                        last = nc.tensor.matmul(bank[6 + vt][:, c * CH:(c + 1) * CH],
                                                states[:, h % 2, c - 1, vt * P:(vt + 1) * P],
                                                qT[:, h, c * CH:(c + 1) * CH], start=False, stop=(c == NCH - 1),
                                                skip_group_check=True)
                last.then_inc(S("o_mm"), 1)

            def gla_square_sum(h):
                pe.wait_ge(S("o_out"), h + 1)
                pe.wait_ge(S("kd_out"), min(h + 2, GH))
                for vt in range(2):
                    last = nc.tensor.matmul(bank[4], ones[:], work[:, vt, 0:NP_TOK], start=(vt == 0), stop=(vt == 1))
                last.then_inc(S("oss_mm"), 1)

            for u in range(8):
                h = u // 2
                product(PHASES["g"][0] + u, 0)
                if u == 0:
                    v_tile(7)
                if u % 2 == 0:
                    if h:
                        gla_output(h - 1)
                    gla_scores(h)
                else:
                    if h:
                        gla_square_sum(h - 1)
                    gla_states(h)
            gla_output(GH - 1)
            gla_square_sum(GH - 1)
            pe.wait_ge(S("o_sqrt"), GH)
            for n in range(NS * GH):
                h = n % GH
                pe.wait_ge(S("key_row"), n // GH + 1)
                if n >= 4:
                    pe.wait_ge(S("s_new"), n - 3)
                nc.tensor.matmul(bank[4 + n % 4][:, 0:HV], attT[0:NS, (n // GH) % 2, h * P:(h + 1) * P],
                                 vs[:, h * HV:(h + 1) * HV], start=True, stop=True).then_inc(S("skv_mm"), 1)
            pe.wait_ge(S("s_new"), NS * GH)
            for h in range(GH):
                for vt in range(2):
                    for b in range(NS):
                        c = (2 * h + vt) * NS + b
                        last = nc.tensor.matmul(bank[4][:, c:c + 1], s0[:, b * GH + h, vt * P:(vt + 1) * P],
                                                qT[:, h, NP_TOK + b:NP_TOK + b + 1], start=True, stop=True)
            last.then_inc(S("so_mm"), 1)
            pe.wait_ge(S("sosq"), 1)
            for vt in range(2):
                last = nc.tensor.matmul(bank[5][:, 0:GH * NS], ones[:],
                                        work[:, 2, 0:2 * GH * NS].rearrange("p (h v b) -> p v h b", h=GH, v=2)[:, vt],
                                        start=(vt == 0), stop=(vt == 1))
            last.then_inc(S("soss_mm"), 1)
            for u in range(2):
                up_product(PHASES["up0"][0] + u, pT_hi, pT_lo, 2)
            for u in range(8):
                product(PHASES["wo0"][0] + u, KT, wait_x=(u == 0))
            for u in range(8):
                product(PHASES["ple0"][0] + u, 2 * KT, wait_x=(u == 0))
                if u == 0:
                    square_sum(1)
            for u in range(8):
                product(PHASES["q1"][0] + u, 3 * KT, wait_x=(u == 0))
                if u == 0:
                    square_sum(2)
            pe.wait_ge(S("evac"), last_tile("q1"))
            for k in range(KT):
                last = nc.tensor.transpose(bank[4 + k // 4][0:NS, (k % 4) * P:(k % 4 + 1) * P], q1T[:, k, NP_TOK:T], ident[:])
            last.then_inc(S("qs_t"), 1)
            pe.wait_ge(S("qs_out"), 1)
            pe.wait_ge(S("bias_row"), 1)
            nc.tensor.matmul(bank[4][:, 0:SH], ones[0:1, :], biasrow[0:1, 0:SH], start=True, stop=True)
            nc.tensor.matmul(bank[5][:, 0:1], biasrow[0:1, :], ones[0:1, 0:1], start=True, stop=True).then_inc(S("bias_mm"), 1)

            def query_everywhere(b):
                if b:
                    pe.wait_ge(S("qb_in"), b)
                for t in range(2):
                    last = nc.tensor.matmul(pp[3][:, t, :], sel[:, b, :], work[0:NS, t, 0:512], start=True, stop=True)
                last.then_inc(S("qb_mm"), 1)

            pe.wait_ge(S("sel"), 1)
            query_everywhere(0)
            query_everywhere(1)
            asked = 2

            def kv_transposes(t):
                pe.wait_ge(S("evac"), PHASES["K"][2] + t + 1)
                pe.wait_ge(S("kv_out"), t) if t else pe.wait_ge(S("bias_out"), 1)
                token_major(K1T[:, t, :] if t < 8 else work[:, 2 + t % 2, :], 4, S("kv_t"))

            for i in range(24):
                product(PHASES["g1"][0] + i, 3 * KT)
                while asked < NS and asked <= (i * K_PER_JOB) // NPG + 1 and i >= 1:
                    query_everywhere(asked)
                    asked += 1
                if i >= KV_LAG + 8:
                    kv_transposes(i - KV_LAG - 8)
            while asked < NS:
                query_everywhere(asked)
                asked += 1
            for t in range(16 - KV_LAG, 16):
                kv_transposes(t)
            pe.wait_ge(S("k_used"), NPAGES)
            for g in range(4):
                for c in range(4):
                    last = nc.tensor.transpose(bank[g][:, c * P:(c + 1) * P], zall[:, g * 4 + c, :], ident[:])
                last.then_inc(S("z_t"), 1)
            pe.wait_ge(S("a_s"), 1)
            for g in range(4):
                for c in range(4):
                    j = g * 4 + c
                    last = nc.tensor.transpose(bank[g][:, c * P:(c + 1) * P], ssig[:, j * P:(j + 1) * P], ident[:])
                last.then_inc(S("a_t"), 1)
            pe.wait_ge(S("a_out"), 4)
            pe.wait_ge(S("kv_out"), 16)
            pe.wait_ge(S("qb_in"), NS)

            def scores(h):
                i, r = h // 2, (h % 2) * HD
                if h:
                    pe.wait_ge(S("sig_p"), h)
                for q in (0, 2, 1, 3):
                    bk, c0 = ZB[q]
                    n = (q + 1) * P
                    nc.tensor.matmul(bank[bk][:, c0:c0 + n], q1T[r:r + HD, i, q * P:(q + 1) * P],
                                     K1T[r:r + HD, i, 0:n], start=True, stop=False, skip_group_check=True)
                    last = nc.tensor.matmul(bank[bk][:, c0 + n - P:c0 + n], identb[:], maskneg[:],
                                            start=False, stop=True, skip_group_check=True)
                last.then_inc(S("z_p"), 1)

            def weights_back(h):
                pe.wait_ge(S("a_p"), h + 1)
                if h:
                    pe.wait_ge(S("at_out"), h)
                for kb in range(TB):
                    bk, c0 = AB[kb]
                    for q in range(kb, TB):
                        last = nc.tensor.transpose(bank[bk][:, c0 + (q - kb) * P:c0 + (q - kb + 1) * P],
                                                   psig[h % 2][:, PSEG[q] + kb * P:PSEG[q] + (kb + 1) * P], ident[:])
                last.then_inc(S("at_t"), 1)

            def values(h):
                r = (h % 2) * HD
                pe.wait_ge(S("at_out"), h + 1)
                if h >= 2 and h % 2 == 0:
                    pe.wait_ge(S("u1_out"), h // 2)
                for kb in range(TB):
                    n = (TB - kb) * P
                    last = nc.tensor.matmul(bank[6][r:r + HD, kb * P:NP_TOK], V1[:, kb, h * HD:(h + 1) * HD],
                                            pat[:, AO[kb]:AO[kb] + n], start=(kb == 0), stop=(kb == TB - 1),
                                            skip_group_check=True)
                last.then_inc(S("o_p"), 1)

            def value_page(n):
                b, j, m = n // NPG, n % NPG, NPAGES + n
                pe.wait_ge(S(f"page_in{m % RING}"), 16 * (m // RING + 1))
                for i in range(KT):
                    c = (b * KT + i) * 2
                    last = nc.tensor.matmul(bank[7][:, c:c + 2], ring[:, m % RING, i * P:(i + 1) * P],
                                            zall[:, j, b * SH + 2 * i:b * SH + 2 * i + 2],
                                            start=(n == 0 and i == 0), stop=(n == NPAGES - 1), skip_group_check=True)
                last.then_inc(S("v_used"), 1)

            scores(0)
            for h in range(SH):
                if h + 1 < SH:
                    scores(h + 1)
                for n in range(4):
                    value_page(h * 8 + n)
                weights_back(h)
                for n in range(4, 8):
                    value_page(h * 8 + n)
                values(h)
            pe.wait_ge(S("p1_in"), 32)
            pe.wait_ge(S("u1_out"), KT)
            for c in range(2):
                for b in range(TB):
                    nc.tensor.transpose(bank[4 + c][:, b * P:(b + 1) * P], pin1[:, b, c * P:(c + 1) * P], ident[:])
                nc.tensor.transpose(bank[(3, 6)[c]][:, 0:NS], ps1[:, c * P:(c + 1) * P],
                                    ident[0:NS, 0:NS]).then_inc(S("pt"), 1)
            for u in range(2):
                up_product(PHASES["up1"][0] + u, pT1_hi, pT1_lo, 4)
            for u in range(8):
                product(PHASES["wo1"][0] + u, 4 * KT, wait_x=(u == 0))
            for u in range(8):
                product(PHASES["ple1"][0] + u, 5 * KT, wait_x=(u == 0))
                if u == 0:
                    square_sum(3)
            square_sum(4)
            for k in range(KT):
                pe.wait_ge(S("y_t"), k + 1)
                if k >= 2:
                    pe.wait_ge(S("y_out"), k - 1)
                src = work[:, 2 + k % 2, :]
                for b in range(TB):
                    nc.tensor.transpose(bank[4 + k % 2][:, b * P:(b + 1) * P], src[:, b * P:(b + 1) * P], ident[:])
                nc.tensor.transpose(bank[6 + k % 2][0:NS, 0:P], src[:, NP_TOK:T], ident[:]).then_inc(S("yt_t"), 1)


KV_LAG = 1

_INS = ['x_prompt', 'x_sample', 'state_gla', 'cache_k', 'cache_v', 'page_table', 'p_prompt', 'p_sample',
        'g_pre', 'w_ple_gate', 'w_ple_up', 'g_ple', 'gla_w_in', 'gla_w_gk2', 'gla_b_gk', 'gla_g_out', 'gla_w_out',
        'g_kv', 'w_kv', 'sb_w_in', 'sb_bias', 'sb_w_out', 'g_final']
_OUTS = [(1, 512, 1024), (8, 1, 1024), (1, 1, 4, 128, 256), (1, 8, 4, 128, 256),
         (1, 512, 16, 64), (1, 512, 16, 64), (8, 1, 16, 64), (8, 1, 16, 64)]


def kernel(**inputs):
    import numpy as _np
    import concourse.bacc as _bacc
    from concourse import mybir as _mybir
    from concourse.bass_utils import run_bass_kernel_spmd as _run

    nc = _bacc.Bacc("TRN2", target_bir_lowering=False, num_devices=1)
    arrays, args = {}, []
    for name in _INS:
        a = _np.ascontiguousarray(inputs[name])
        arrays[f"in_{name}_dram"] = a
        args.append(nc.dram_tensor(f"in_{name}_dram", a.shape, _mybir.dt.from_np(a.dtype), kind="ExternalInput").ap())
    for i, shape in enumerate(_OUTS):
        args.append(nc.dram_tensor(f"out_{i}_dram", shape, F32, kind="ExternalOutput").ap())
    build(nc, *args)
    r = _run(nc, [arrays], core_ids=[0])
    return tuple(r.results[0][f"out_{i}_dram"] for i in range(len(_OUTS)))
```

```python
import concourse.bass as bass
from concourse import mybir
from contextlib import ExitStack

F32 = mybir.dt.float32
F32R = mybir.dt.float32r
BF16 = mybir.dt.bfloat16
I32 = mybir.dt.int32
ALU = mybir.AluOpType
ACT = mybir.ActivationFunctionType
AX = mybir.AxisListType

P = 128
D = 1024
KT = D // P
NP_TOK = 512
NS = 8
T = NP_TOK + NS
H2 = T // 2
TB = NP_TOK // P
PLE = 256
EPS = 1e-6
GH, HK, HV = 4, 128, 256
CH = 64
NCH = NP_TOK // CH
RANK = 16
GATE_NORM = 16.0
SH, HD = 16, 64
NPG = 16
PAST = P * NPG
NPAGES = NS * NPG
NEG = -1e30

PHASES = {}
_j = _m = 0
for _name, _n, _per in (("gk", 2, 1), ("q", 4, 1), ("k", 4, 1), ("v", 8, 1), ("g", 8, 1), ("up0", 2, 4),
                        ("wo0", 8, 1), ("ple0", 8, 1), ("q1", 8, 1), ("g1", 8, 1), ("K", 8, 1), ("V", 8, 1),
                        ("up1", 2, 4), ("wo1", 8, 1), ("ple1", 8, 1)):
    PHASES[_name] = (_j, _n, _m)
    _j += _n
    _m += 1 if _name == "gk" else _n * _per
NJOBS = _j
GFINAL, GOUT, BGK, NVEC = 40, 48, 50, 54
GAIN = {"gk": 0, "q": 0, "k": 0, "v": 0, "g": 0, "up0": None, "wo0": GOUT, "ple0": 16, "q1": 8, "g1": 8,
        "K": 32, "V": 32, "up1": None, "wo1": None, "ple1": 24}
K_PER_JOB = 4
K_JOBS = 24 * K_PER_JOB
EARLY = 6
POOL_SHARE = ((0, 1, 3, 4, 6, 7, 9), (0, 1, 2, 4, 5, 6, 7, 9))
POOL_LO = (1, 4, 6)
RING = 6
VRING, VHI = 7, 4
ZW = NPG * 2 * P + 96
ZB = {0: (0, 0), 2: (0, P), 1: (1, 0), 3: (2, 0)}
PSEG = {0: 0, 2: 128, 1: 512, 3: 768}
SEG = {0: 0, 2: 129, 1: 514, 3: 771}
NZ = P * (1 + 2 + 3 + 4)
AB = {0: (3, 0), 1: (4, 0), 3: (4, 384), 2: (1, 256)}
AO = {0: 0, 1: 512, 3: 896, 2: 1024}


def phase_of(job):
    for name, (j0, n, m0) in PHASES.items():
        if j0 <= job < j0 + n:
            return name
    raise ValueError(job)


def tiles_through(job):
    if job < PHASES["q"][0]:
        return 1
    name = phase_of(job)
    j0, _, m0 = PHASES[name]
    return m0 + (job - j0 + 1) * (4 if name[:2] == "up" else 1)


def gains_through(pair):
    return sum(GAIN[phase_of(2 * p)] is not None for p in range(pair + 1))


def on_pool(n):
    return n % 10 in POOL_SHARE[n >= K_JOBS]


def pool_pages(n):
    return sum(on_pool(i) for i in range(n))


def early_pages(h):
    left = NPAGES - K_JOBS
    return range(K_JOBS + left * h // EARLY, K_JOBS + left * (h + 1) // EARLY)


def pool_lo(n):
    return sum(i % 8 in POOL_LO for i in range(n))


class Steps:

    def __init__(self, engine, sem):
        self.engine, self.sem, self.n = engine, sem, 0

    def did(self, ins):
        self.n += 1
        ins.then_inc(self.sem, 1)

    def wait(self):
        self.engine.wait_ge(self.sem, self.n)

    def then(self, ins):
        self.did(ins)
        self.wait()


def build(nc, x_prompt, x_sample, state_gla, cache_k, cache_v, page_table, p_prompt, p_sample,
          g_pre, w_ple_gate, w_ple_up, g_ple, gla_w_in, gla_w_gk2, gla_b_gk, gla_g_out, gla_w_out,
          g_kv, w_kv, sb_w_in, sb_bias, sb_w_out, g_final,
          y_prompt, y_sample, st_prompt, st_sample, k_prompt, v_prompt, k_sample, v_sample):
    with ExitStack() as ctx:
        top = [(nc.sbuf_base + 63) // 64 * 64]

        def at(name, shape, dt, offset):
            return nc.alloc_sbuf_tensor_at(name, shape, dt, offset=offset)

        def size(shape, dt=F32):
            n = 2 if dt == BF16 else 4
            for s in shape[1:]:
                n *= s
            return (n + 63) // 64 * 64

        def new(name, shape, dt=F32):
            t = at(name, shape, dt, top[0])
            top[0] += size(shape, dt)
            assert top[0] <= nc.sbuf_usable_end, (name, top[0] - nc.sbuf_usable_end)
            return t

        hT = new("hT", [P, KT, T])
        offA = top[0]
        xa_hi, xa_lo = new("xa_hi", [P, KT, T], F32R), new("xa_lo", [P, KT, T], F32R)
        offB = top[0]
        xb_hi, xb_lo = new("xb_hi", [P, KT, T], F32R), new("xb_lo", [P, KT, T], F32R)
        off_raw = top[0]
        w_raw = new("w_raw", [P, 2, 2048])
        w_hi = [new(f"w_hi{i}", [P, 1024], F32R) for i in range(2)]
        w_lo = [new(f"w_lo{i}", [P, 1024], F32R) for i in range(2)]
        off_work = top[0]
        work = new("work", [P, 4, T])
        sqacc = new("sqacc", [P, T])
        rstd = new("rstd", [P, T])
        ident = new("ident", [P, P])
        ones = new("ones", [P, P])
        identb = new("identb", [P, P], BF16)
        maskneg = new("maskneg", [P, P], BF16)
        vrows = new("vrows", [NVEC, P])
        gcol = new("gcol", [P, NVEC])
        epsc = new("epsc", [P, 1])
        biasrow = new("biasrow", [1, P])
        biasbc = new("biasbc", [P, SH])
        nbiasbc = new("nbiasbc", [P, SH])
        biascol = new("biascol", [P, 1])
        nbiascol = new("nbiascol", [P, 1])
        ptab = new("ptab", [1, NPAGES], I32)
        off_phase = top[0]
        qT = new("qT", [P, GH, T])
        kT = new("kT", [P, GH, T])
        gkT = new("gkT", [P, GH, T])
        gT = new("gT", [P, KT, T])
        vtok = new("vtok", [P, TB, D])
        vs = new("vs", [NS, D])
        pT_hi, pT_lo = new("pT_hi", [P, 2, T], F32R), new("pT_lo", [P, 2, T], F32R)
        k_s = new("k_s", [NS, GH * HK])
        chmask = new("chmask", [P, NP_TOK])
        attmask = new("attmask", [P, P])
        dec = new("dec", [P, GH, NCH])
        w2 = new("w2", [RANK, GH * HK])
        ps0 = new("ps0", [NS, PLE])
        kb8 = size([P, GH, NP_TOK])
        kdtok = at("kdtok", [P, GH, TB, P], F32, offB)
        attT = at("attT", [P, GH, NP_TOK], F32, offB + kb8)
        gE = at("gE", [P, GH, NP_TOK], F32, offB + 2 * kb8)
        gD = at("gD", [P, GH, NP_TOK], F32, offB + 3 * kb8)
        states = at("states", [P, 2, NCH, HV], F32, offB + 2 * kb8)
        s0 = at("s0", [P, NS * GH, HV], F32, offA)
        up0T = at("up0T", [P, KT, T], F32, off_phase)
        end_a, top[0] = top[0], off_phase
        q1T = new("q1T", [P, KT, T])
        K1T = new("K1T", [P, KT, T])
        g1T = new("g1T", [P, KT, T])
        V1 = new("V1", [P, TB, D])
        qb = new("qb", [P, 2, D])
        sel = new("sel", [NS, NS, P])
        up1T = at("up1T", [P, KT, T], F32, off_phase)
        o1 = off_phase + size([P, KT, T])
        pT1_hi = at("pT1_hi", [P, 2, T], F32R, o1)
        pT1_lo = at("pT1_lo", [P, 2, T], F32R, o1 + size([P, 2, T]))
        pin1 = at("pin1", [P, TB, PLE], F32, o1 + 2 * size([P, 2, T]))
        ps1 = at("ps1", [NS, PLE], F32, o1 + 2 * size([P, 2, T]) + size([P, TB, PLE]))
        ystage = at("ystage", [P, TB, D], F32, o1 + size([P, KT, T]))
        ysrow = at("ysrow", [NS, D], F32, o1)
        ring = at("ring", [P, RING, D], F32, offA)
        zall = at("zall", [P, NPG, P], F32, offA + RING * D * 4)
        zs = at("zs", [P, ZW], F32R, offA + 4 * D * 4)
        bmask, ob = qb[:, 0, :], qb[:, 1, :]
        ssig = at("ssig", [P, PAST], F32, off_raw + PAST * 4)
        scum = at("scum", [P, PAST + 1], F32, off_work)
        pz = size([P, NZ + 4])
        psig = [at(f"psig{i}", [P, NZ], F32, offB + i * pz) for i in range(2)]
        pcum = [at(f"pcum{i}", [P, NZ + 4], F32, offB + (2 + i) * pz) for i in range(2)]
        pat = at("pat", [P, NZ], F32, offB + 4 * pz)
        vslot = [at(f"vslot{i}", [P, D], F32, o) for i, o in enumerate(
            [offA + i * D * 4 for i in range(4)] + [offB + 4 * pz + size([P, NZ])] +
            [off_raw + PAST * 4 + i * D * 4 for i in range(2)])]
        vlo = [at(f"vlo{i}", [P, D], F32R, o) for i, o in enumerate(
            [offA + i * D * 4 for i in range(4)] + [offB + 4 * pz + size([P, NZ])] +
            [off_raw + PAST * 4 + i * D * 4 for i in range(2)])]
        vhi = [w_hi[0], w_hi[1], w_lo[0], w_lo[1]]

        pp = [ctx.enter_context(nc.psum_tensor(f"pp{i}", [P, 2, 512], F32)) for i in range(4)]
        bank = [pp[i // 2][:, i % 2, :] for i in range(8)]

        def chunk_bank(c):
            return bank[6 + c % 2][:, (c // 2 % 2) * HV:(c // 2 % 2 + 1) * HV]

        def weight_part(g, part):
            return zs[:, 0:NPG * 2 * P].rearrange("p (j b e h) -> p j b e h", b=NS, e=2, h=SH)[:, 4 * g:4 * g + 4, :, part, :]

        sems = {}

        def S(name):
            if name not in sems:
                sems[name] = ctx.enter_context(nc.semaphore(name))
            return sems[name]

        block = ctx.enter_context(nc.Block())

        def weight_pair_source(p):
            name = phase_of(2 * p)
            o = (2 * p - PHASES[name][0]) * P
            w, c0 = {"q": (gla_w_in[0], 0), "k": (gla_w_in[0], 512), "v": (gla_w_in[0], 1024),
                     "g": (gla_w_in[0], 2048), "wo0": (gla_w_out[0], 0), "ple0": (w_ple_gate[0], 0),
                     "q1": (sb_w_in[0], 0), "g1": (sb_w_in[0], D), "K": (w_kv, 0), "V": (w_kv, D),
                     "wo1": (sb_w_out[0], 0), "ple1": (w_ple_gate[1], 0)}[name]
            return w.rearrange("(k p) n -> p k n", p=P)[:, :, c0 + o:c0 + o + 2 * P]

        def raw_pair(p):
            name = phase_of(2 * p)
            return w_raw[:, p % 2, :].rearrange("p (k n) -> p k n", k=2 if name[:2] == "up" else KT)

        def split_views(j):
            k = 2 if phase_of(j)[:2] == "up" else KT
            n = 1024 // k
            return (raw_pair(j // 2)[:, :, n * (j % 2):n * (j % 2) + n],
                    w_hi[j % 2][:].rearrange("p (k n) -> p k n", k=k),
                    w_lo[j % 2][:].rearrange("p (k n) -> p k n", k=k))

        def x_parts(n):
            hi, lo = (xa_hi, xa_lo) if "ABABBA"[n // KT] == "A" else (xb_hi, xb_lo)
            return hi[:, n % KT, :], lo[:, n % KT, :]

        def last_tile(name):
            j0, n, _ = PHASES[name]
            return tiles_through(j0 + n - 1)

        @block.sync
        def _(sp):
            for r0, n, v in ((0, 16, g_pre), (16, 16, g_ple), (32, 8, g_kv), (GFINAL, 8, g_final),
                             (GOUT, 2, gla_g_out), (BGK, 4, gla_b_gk)):
                flat = v if len(v.shape) == 1 else v.rearrange("a b -> (a b)")
                sp.dma_start(vrows[r0:r0 + n, :], flat.rearrange("(r c) -> r c", c=P)).then_inc(S("vec_in"), 16)
            sp.dma_start(vtok[:, :, :], x_prompt[0].rearrange("(b p) d -> p b d", p=P)).then_inc(S("x_in"), 16)
            sp.dma_start(vs[:, :], x_sample[:, 0, :]).then_inc(S("x_in"), 16)
            sp.wait_ge(S("raw_zero"), 1)
            sp.dma_start(raw_pair(0)[:, :, 0:RANK],
                         gla_w_in[0].rearrange("(k p) n -> p k n", p=P)[:, :, 3072:3072 + RANK]).then_inc(S("w_in0"), 16)
            sp.dma_start(gT[:, 0:TB, 0:PLE], p_prompt[0, 0].rearrange("(b p) d -> p b d", p=P)).then_inc(S("p_in"), 16)
            sp.dma_start(ps0[:, :], p_sample[0, :, 0, :]).then_inc(S("p_in"), 16)
            sp.dma_start(w2[:, :], gla_w_gk2[0]).then_inc(S("w2_in"), 16)
            sp.dma_start(ptab[0:1, :], page_table.rearrange("b n -> (b n)").rearrange("(o n) -> o n", o=1)).then_inc(S("ptab_in"), 16)
            sp.dma_start(biasrow[0:1, 0:SH], sb_bias).then_inc(S("bias_in"), 16)

            def load_pair(p):
                if p >= 2:
                    sp.wait_ge(S("w_split"), 2 * (p - 1))
                src = (w_ple_up[int(phase_of(2 * p)[2])].rearrange("(k p) n -> p k n", p=P)
                       if phase_of(2 * p)[:2] == "up" else weight_pair_source(p))
                sp.dma_start(raw_pair(p), src).then_inc(S(f"w_in{p % 2}"), 16)

            def load_page(n):
                idx = sp.value_load(ptab[0:1, n % NPAGES:n % NPAGES + 1], min_val=0, max_val=cache_k.shape[0] - 1)
                if n < NPAGES:
                    if n >= RING:
                        sp.wait_ge(S("k_used"), n - RING + 1)
                    dst, arrived, src = ring[:, n % RING, :], S(f"page_in{n % RING}"), cache_k
                else:
                    m = n - NPAGES
                    if m < 4:
                        sp.wait_ge(S("k_used"), max(i for i in range(NPAGES) if i % RING == m) + 1)
                    elif m == 4:
                        sp.wait_ge(S("mm"), last_tile("V"))
                    elif m < VRING:
                        sp.wait_ge(S("a_t"), 4)
                    else:
                        sp.wait_ge(S("v_used"), m - VRING + 1)
                    dst, arrived, src = vslot[m % VRING][:], S(f"v_in{m % VRING}"), cache_v
                sp.dma_start(dst, src[bass.ds(idx, 1)].rearrange("o t h d -> (o t) (h d)")).then_inc(arrived, 16)

            q1 = PHASES["q1"][0] // 2
            for p in range(1, q1):
                load_pair(p)
                if 2 * p == PHASES["up0"][0] + 2:
                    sp.wait_ge(S("mm"), last_tile("g"))
                    sp.dma_start(s0[:, :, :], state_gla[0].rearrange("b h k v -> k (b h) v")).then_inc(S("s0_in"), 16)
            g1, up1 = PHASES["g1"][0] // 2, PHASES["up1"][0] // 2
            for p in range(q1, g1 + 2):
                load_pair(p)
            sp.wait_ge(S("ptab_in"), 16)
            sp.wait_ge(S("mm"), last_tile("ple0"))
            for n in range(RING):
                load_page(n)
            n = RING
            for p in range(g1, up1):
                if p + 2 <= up1:
                    load_pair(p + 2)
                while n < min(NPAGES, RING + 2 * K_PER_JOB * (p + 1 - g1)):
                    load_page(n)
                    n += 1
            while n < 2 * NPAGES:
                load_page(n)
                n += 1
            sp.wait_ge(S("z_p"), SH)
            sp.dma_start(pin1[:, :, :], p_prompt[1, 0].rearrange("(b p) d -> p b d", p=P)).then_inc(S("p1_in"), 16)
            sp.dma_start(ps1[:, :], p_sample[1, :, 0, :]).then_inc(S("p1_in"), 16)
            sp.wait_ge(S("v_used"), NPAGES)
            for p in range(up1 + 1, NJOBS // 2):
                load_pair(p)
            for k in range(KT):
                sp.wait_ge(S("y_out"), k + 1)
                sp.dma_start(y_prompt[0].rearrange("(b p) d -> p b d", p=P)[:, :, k * P:(k + 1) * P],
                             ystage[:, :, k * P:(k + 1) * P]).then_inc(S("results"), 16)
            sp.dma_start(y_sample[:, 0, :], ysrow[:, :]).then_inc(S("results"), 16)
            sp.wait_ge(S("results"), 16 * (KT + 1))
            for e in range(2):
                sp.wait_ge(S(f"st_out{e}"), 16 * GH // 2)
            sp.wait_ge(S("ss_out"), 16)
            sp.wait_ge(S("kv_ss"), 16 * 4)
            for e in range(4):
                sp.wait_ge(S(f"k_st{e}"), 16 * KT // 4)
            sp.wait_ge(S("v_st"), 16)

        @block.gpsimd
        def _(pool):
            own = Steps(pool, S("pool_steps"))
            nc.gpsimd.memset(w_raw[:, 0, :], 0.0).then_inc(S("raw_zero"), 1)
            nc.gpsimd.memset(attmask[:], 1.0)
            nc.gpsimd.memset(chmask[:], 1.0)
            nc.gpsimd.memset(maskneg[:], NEG)
            own.then(nc.gpsimd.memset(ident[:], 0.0))
            nc.gpsimd.affine_select(out=ident[:], in_=ident[:], compare_op=ALU.not_equal, fill=1.0, base=0,
                                    pattern=[[-1, P]], channel_multiplier=1).then_inc(S("ident"), 1)
            pool.wait_ge(S("ident"), 1)
            nc.gpsimd.tensor_copy(identb[:], ident[:])
            nc.gpsimd.affine_select(out=maskneg[:], in_=maskneg[:], compare_op=ALU.is_ge, fill=0.0, base=0,
                                    pattern=[[1, P]], channel_multiplier=-1)
            nc.gpsimd.memset(chmask[:, 0:NP_TOK:CH], 0.0)
            own.then(nc.gpsimd.memset(attmask[0:CH, CH:P], 0.0))
            nc.gpsimd.affine_select(out=attmask[:], in_=attmask[:], compare_op=ALU.is_ge, fill=0.0, base=0,
                                    pattern=[[1, P]], channel_multiplier=-1)
            nc.gpsimd.memset(attT[:], 0.0)
            nc.gpsimd.memset(ones[:], 1.0)
            nc.gpsimd.memset(epsc[:], EPS).then_inc(S("consts"), 1)

            def scale_pair(p):
                if p >= NJOBS // 2 or GAIN[phase_of(2 * p)] is None:
                    return
                g0 = GAIN[phase_of(2 * p)]
                pool.wait_ge(S(f"w_in{p % 2}"), 16 * (p // 2 + 1))
                if p == 0:
                    pool.wait_ge(S("gcol"), 1)
                v = raw_pair(p)
                if g0 == GOUT:
                    v = v.rearrange("p (a c) n -> p a c n", c=2)
                    g = gcol[:, g0:g0 + 2].unsqueeze(1).unsqueeze(3).to_broadcast([P, GH, 2, 2 * P])
                else:
                    g = gcol[:, g0:g0 + KT].unsqueeze(2).to_broadcast([P, KT, 2 * P])
                nc.gpsimd.tensor_tensor(v, v, g, ALU.mult).then_inc(S("w_scaled"), 1)

            def sum_squares(n):
                pool.wait_ge(S("sq"), n + 1)
                if n % KT == 0:
                    if n:
                        pool.wait_ge(S("ss_mm"), n // KT)
                    if n == 3 * KT:
                        pool.wait_ge(S("kv_ss"), 64)
                    nc.gpsimd.tensor_copy(sqacc[:], work[:, n % 2, :]).then_inc(S("sq_added"), 1)
                else:
                    pool.wait_ge(S("sq_added"), n)
                    nc.gpsimd.tensor_tensor(sqacc[:], sqacc[:], work[:, n % 2, :], ALU.add).then_inc(S("sq_added"), 1)

            def multiply_page(n):
                pool.wait_ge(S("qb_in"), n // NPG + 1)
                pool.wait_ge(S(f"page_in{n % RING}"), 16 * (n // RING + 1))
                nc.gpsimd.tensor_tensor(ring[:, n % RING, :], ring[:, n % RING, :], qb[:, (n // NPG) % 2, :],
                                        ALU.mult).then_inc(S("k_mul_pool"), 1)

            scale_pair(0)
            scale_pair(1)
            for n in range(KT):
                sum_squares(n)
            for p in range(2, PHASES["wo0"][0] // 2 + 2):
                scale_pair(p)
            for i, (name, h) in enumerate((("wo0", 1), ("ple0", 2))):
                for u in range(8):
                    sum_squares(h * KT + u)
                    if u % 2 == 0:
                        scale_pair(PHASES[name][0] // 2 + 2 + u // 2)
            for u in range(4):
                scale_pair(PHASES["q1"][0] // 2 + 2 + u)
            pool.wait_ge(S("evac"), last_tile("ple0") + 1)
            own.then(nc.gpsimd.memset(sel[:], 0.0))
            nc.gpsimd.affine_select(out=sel[:], in_=sel[:], compare_op=ALU.not_equal, fill=1.0, base=0,
                                    pattern=[[-1, NS], [0, P]], channel_multiplier=1).then_inc(S("sel"), 1)
            n = 0
            for i in range(24):
                for _ in range(K_PER_JOB):
                    if on_pool(n):
                        multiply_page(n)
                    n += 1
                if i % 2 == 0:
                    scale_pair(PHASES["g1"][0] // 2 + 2 + i // 2)
            while n < NPAGES:
                if on_pool(n):
                    multiply_page(n)
                n += 1
            pool.wait_ge(S("k_used"), NPAGES)
            own.then(nc.gpsimd.memset(bmask, 0.0))
            part = bmask.rearrange("p (h d) -> p h d", d=HD)
            own.then(nc.gpsimd.affine_select(out=part, in_=part, compare_op=ALU.not_equal, fill=1.0, base=0,
                                             pattern=[[1, SH], [0, HD]], channel_multiplier=-1))
            nc.gpsimd.affine_select(out=part, in_=part, compare_op=ALU.not_equal, fill=1.0, base=SH,
                                    pattern=[[1, SH], [0, HD]], channel_multiplier=-1).then_inc(S("bmask"), 1)
            pool.wait_ge(S("z_t"), 4)
            nc.gpsimd.memset(zs[:, NPG * 2 * P:ZW].bitcast(F32), 0.0).then_inc(S("zs_pad"), 1)
            for m in range(NPAGES):
                if m % 8 in POOL_LO:
                    pool.wait_ge(S("v_hi"), m + 1)
                    v = vslot[m % VRING]
                    nc.gpsimd.tensor_tensor(vlo[m % VRING][:], v[:], vhi[m % VHI][:].bitcast(F32),
                                            ALU.subtract).then_inc(S("v_lo_pool"), 1)
            for i, name in enumerate(("wo1", "ple1")):
                for u in range(8):
                    sum_squares((3 + i) * KT + u)
                    if u % 2 == 0:
                        scale_pair(PHASES[name][0] // 2 + 2 + u // 2)

        @block.scalar
        def _(act):
            own = Steps(act, S("act_steps"))
            act.wait_ge(S("consts"), 1)
            act.wait_ge(S("gcol_t"), 1)
            nc.scalar.copy(gcol[:], bank[7][:, 0:NVEC]).then_inc(S("gcol"), 1)

            def split_hi(j):
                if j >= NJOBS:
                    return
                p = j // 2
                if GAIN[phase_of(j)] is None:
                    act.wait_ge(S(f"w_in{p % 2}"), 16 * (p // 2 + 1))
                else:
                    act.wait_ge(S("w_scaled"), gains_through(p))
                if j >= 2:
                    act.wait_ge(S("mm"), tiles_through(j - 2))
                if j == 3:
                    act.wait_ge(S("w_split"), 2)
                raw, hi, _ = split_views(j)
                nc.scalar.copy(hi, raw).then_inc(S("w_hi"), 1)

            def x_hi(n, src):
                nc.scalar.copy(x_parts(n)[0], src).then_inc(S("x_hi"), 1)

            def square(n, src):
                if n >= 2:
                    act.wait_ge(S("sq_added"), n - 1)
                nc.scalar.activation(work[:, n % 2, :], src, ACT.Square).then_inc(S("sq"), 1)

            def rms(i):
                act.wait_ge(S("ss_mm"), i + 1)
                nc.scalar.activation(rstd[:].rearrange("p (t n) -> p t n", t=2), pp[3][:, :, 0:H2], ACT.Sqrt,
                                     bias=epsc[:], scale=1.0 / D).then_inc(S("r_sqrt"), 1)

            def sigmoid_tile(n, src, dst):
                nc.scalar.activation(dst, src, ACT.Sigmoid).then_inc(S("sigm"), 1)

            for k in range(KT):
                act.wait_ge(S("xt"), k + 1)
                nc.scalar.copy(hT[:, k, 0:NP_TOK], bank[4 + k % 2])
                own.did(nc.scalar.copy(hT[:, k, NP_TOK:T], bank[6 + k % 2][:, 64:64 + NS]))
                own.wait()
                x_hi(k, hT[:, k, :])
                square(k, hT[:, k, :])
            split_hi(0)
            for c in range(2):
                act.wait_ge(S("pt"), c + 1)
                nc.scalar.copy(pT_hi[:, c, 0:NP_TOK], bank[4 + c])
                nc.scalar.copy(pT_hi[:, c, NP_TOK:T], bank[6 + c][:, 64:64 + NS]).then_inc(S("pt_hi"), 1)
            split_hi(1)
            rms(0)
            for u in range(4):
                split_hi(PHASES["q"][0] + u)
            split_hi(PHASES["k"][0])
            for h in range(GH):
                act.wait_ge(S("gk_out"), h + 1)
                own.then(nc.scalar.activation(gE[:, h, :], gkT[:, h, 0:NP_TOK], ACT.Abs))
                own.then(nc.scalar.activation(gE[:, h, :], gE[:, h, :], ACT.Exp, scale=-1.0))
                nc.scalar.activation(gE[:, h, :], gE[:, h, :], ACT.Ln, bias=1.0)
                own.then(nc.scalar.activation(gD[:, h, 0:NS], gkT[:, h, NP_TOK:T], ACT.Abs))
                own.then(nc.scalar.activation(gD[:, h, 0:NS], gD[:, h, 0:NS], ACT.Exp, scale=-1.0))
                nc.scalar.activation(gD[:, h, 0:NS], gD[:, h, 0:NS], ACT.Ln, bias=1.0).then_inc(S("gk_ln"), 1)
                split_hi(PHASES["k"][0] + h + 1)

            def v_rows(u):
                act.wait_ge(S("v_t"), u + 1)
                nc.scalar.copy(vtok[:, :, u * P:(u + 1) * P], bank[4].rearrange("p (b n) -> p b n", b=TB))
                nc.scalar.copy(vs[:, u * P:(u + 1) * P], bank[5][0:NS, 0:P]).then_inc(S("v_out"), 1)

            for u in range(8):
                split_hi(PHASES["v"][0] + u + 1)
                if u == 0:
                    act.wait_ge(S("ks_t"), 1)
                    nc.scalar.copy(k_s[:], bank[4][0:NS, :]).then_inc(S("ks_out"), 1)
                else:
                    v_rows(u - 1)
                if 1 <= u <= 4:
                    h = u - 1
                    act.wait_ge(S("gk_d"), h + 1)
                    nc.scalar.activation(dec[:, h, :], gkT[:, h, CH - 1:NP_TOK:CH], ACT.Exp, scale=1 / GATE_NORM)
                    nc.scalar.activation(gE[:, h, :], gkT[:, h, 0:NP_TOK], ACT.Exp, scale=1 / GATE_NORM)
                    own.did(nc.scalar.activation(gkT[:, h, NP_TOK:T], gkT[:, h, NP_TOK:T], ACT.Exp, scale=1 / GATE_NORM))
                    nc.scalar.activation(gD[:, h, :], gD[:, h, :], ACT.Exp, scale=1 / GATE_NORM)
                    own.wait()
                    nc.scalar.activation(gkT[:, h, 0:NP_TOK], gkT[:, h, 0:NP_TOK], ACT.Exp,
                                         scale=-1 / GATE_NORM).then_inc(S("gk_e"), 1)

            def o_copies(h):
                act.wait_ge(S("o_mm"), h + 1)
                if h:
                    act.wait_ge(S("oss_mm"), h)
                nc.scalar.copy(qT[:, h, 0:NP_TOK], bank[6])
                nc.scalar.copy(kT[:, h, 0:NP_TOK], bank[7])
                nc.scalar.activation(work[:, 0, 0:NP_TOK], bank[6], ACT.Square)
                nc.scalar.activation(work[:, 1, 0:NP_TOK], bank[7], ACT.Square).then_inc(S("o_out"), 1)
                act.dma_start(st_prompt[0, 0, h], states[:, h % 2, NCH - 1, :]).then_inc(S(f"st_out{h % 2}"), 16)

            def o_rms(h):
                act.wait_ge(S("oss_mm"), h + 1)
                nc.scalar.activation(gkT[:, h, 0:NP_TOK], bank[4], ACT.Sqrt, bias=epsc[:],
                                     scale=1.0 / HV).then_inc(S("o_sqrt"), 1)

            for u in range(8):
                h = u // 2
                split_hi(PHASES["g"][0] + u + 1)
                if u == 0:
                    v_rows(7)
                if u >= 2:
                    act.wait_ge(S("silu"), u - 1)
                act.wait_ge(S("evac"), PHASES["g"][2] + u + 1)
                sigmoid_tile(u, gT[:, u, :], work[:, 2 + u % 2, :])
                if u % 2 == 0:
                    if h:
                        o_copies(h - 1)
                    act.wait_ge(S("kd_t"), h + 1)
                    nc.scalar.copy(kdtok[:, h].rearrange("p b n -> p (b n)"), bank[4]).then_inc(S("kd_out"), 1)
                elif h:
                    o_rms(h - 1)
            o_copies(GH - 1)
            split_hi(PHASES["up0"][0] + 1)
            o_rms(GH - 1)
            act.wait_ge(S("s_new"), NS * GH)
            act.dma_start(st_sample[0].rearrange("b h k v -> k (b h) v"), s0[:, :, :]).then_inc(S("ss_out"), 16)
            act.wait_ge(S("so_mm"), 1)
            nc.scalar.activation(work[:, 2, 0:64], bank[4][:, 0:64], ACT.Square).then_inc(S("sosq"), 1)
            act.wait_ge(S("soss_mm"), 1)
            nc.scalar.activation(work[:, 3, 0:32], bank[5][:, 0:32], ACT.Sqrt, bias=epsc[:],
                                 scale=1.0 / HV).then_inc(S("so_sqrt"), 1)
            act.wait_ge(S("so_used"), 1)
            split_hi(PHASES["up0"][0] + 2)
            for e in range(2):
                act.wait_ge(S(f"st_out{e}"), 16 * GH // 2)
            for i in range(KT):
                x_hi(KT + i, gT[:, i, :])
            for u in range(8):
                j = PHASES["wo0"][0] + u
                split_hi(j + 1)
                if u == 0:
                    act.wait_ge(S("ss_out"), 16)
                act.wait_ge(S("evac"), tiles_through(j))
                x_hi(2 * KT + u, hT[:, u, :])
                square(KT + u, hT[:, u, :])
            for u in range(8):
                j = PHASES["ple0"][0] + u
                split_hi(j + 1)
                if u == 0:
                    rms(1)
                act.wait_ge(S("evac"), tiles_through(j))
                sigmoid_tile(8 + u, work[:, 2 + u % 2, :], work[:, 2 + u % 2, :])
                act.wait_ge(S("h_new"), u + 1)
                x_hi(3 * KT + u, hT[:, u, :])
                square(2 * KT + u, hT[:, u, :])
            for u in range(8):
                j = PHASES["q1"][0] + u
                split_hi(j + 1)
                if u == 0:
                    rms(2)
            act.wait_ge(S("qs_t"), 1)
            qs = work[0:NS, 0:2, 0:512]
            nc.scalar.copy(qs, pp[2][0:NS, :, :]).then_inc(S("qs_out"), 1)

            def query_out(b):
                act.wait_ge(S("qb_mm"), b + 1)
                if b >= 2:
                    act.wait_ge(S("k_used"), (b - 1) * NPG)
                nc.scalar.copy(qb[:, b % 2, :].rearrange("p (t n) -> p t n", t=2), pp[3][:, :, :]).then_inc(S("qb_in"), 1)

            act.wait_ge(S("bias_mm"), 1)
            nc.scalar.copy(biasbc[:], bank[4][:, 0:SH])
            nc.scalar.activation(nbiasbc[:], bank[4][:, 0:SH], ACT.Copy, scale=-1.0)
            nc.scalar.copy(biascol[:], bank[5][:, 0:1])
            nc.scalar.activation(nbiascol[:], bank[5][:, 0:1], ACT.Copy, scale=-1.0).then_inc(S("bias_out"), 1)

            query_out(0)
            query_out(1)
            asked = 2

            def kv_tile(t):
                u = t % 8
                dst = V1[:, :, u * P:(u + 1) * P]
                if t >= 8:
                    act.wait_ge(S(f"k_st{u % 4}"), 32)
                act.wait_ge(S("kv_t"), t + 1)
                nc.scalar.copy(dst, bank[4].rearrange("p (b n) -> p b n", b=TB))
                if t % 4 == 0 and t:
                    act.wait_ge(S("kv_ss"), 16 * (t // 4))
                nc.scalar.copy(sqacc[0:NS, (t % 4) * P:(t % 4 + 1) * P], bank[5][0:NS, 0:P]).then_inc(S("kv_out"), 1)
                act.wait_ge(S("kv_out"), t + 1)
                if t < 8:
                    act.dma_start(k_prompt[0].rearrange("(b p) h d -> p b (h d)", p=P)[:, :, u * P:(u + 1) * P],
                                  dst).then_inc(S(f"k_st{u % 4}"), 16)
                if t % 4 == 3:
                    out = (k_sample if t < 8 else v_sample)[:, 0].rearrange("b h d -> b (h d)")
                    c0 = (u - 3) * P
                    act.dma_start(out[:, c0:c0 + 512], sqacc[0:NS, 0:512]).then_inc(S("kv_ss"), 16)
                if t == 15:
                    act.dma_start(v_prompt[0].rearrange("(b p) h d -> p b (h d)", p=P), V1[:, :, :]).then_inc(S("v_st"), 16)

            for i in range(24):
                j = PHASES["g1"][0] + i
                if i < 23:
                    split_hi(j + 1)
                if i < 8:
                    act.wait_ge(S("evac"), tiles_through(j))
                    if i >= 2:
                        act.wait_ge(S("silu"), 8 + i - 1)
                    sigmoid_tile(16 + i, g1T[:, i, :], work[:, 2 + i % 2, :])
                while asked < NS and asked <= (i * K_PER_JOB) // NPG + 1 and i >= 1:
                    query_out(asked)
                    asked += 1
                if i >= KV_LAG + 8:
                    kv_tile(i - KV_LAG - 8)
            while asked < NS:
                query_out(asked)
                asked += 1
            for t in range(16 - KV_LAG, 16):
                kv_tile(t)

            def sample_sigmoids(g):
                act.wait_ge(S("z_t"), g + 1)
                c = slice(g * 512, (g + 1) * 512)
                nc.scalar.activation(scum[:, c], bank[6 + g % 2], ACT.Sigmoid, bias=nbiascol[:], scale=-HD ** -0.5)
                nc.scalar.activation(ssig[:, c], bank[6 + g % 2], ACT.Sigmoid, bias=biascol[:],
                                     scale=HD ** -0.5).then_inc(S("s_sig"), 1)

            def sample_weights_hi(g):
                act.wait_ge(S("a_t"), g + 1)
                nc.scalar.copy(weight_part(g, 0), bank[6 + g % 2].rearrange("p (j b h) -> p j b h", j=4, b=NS)).then_inc(S("zs_hi"), 1)

            def head_sigmoids(h):
                act.wait_ge(S("z_p"), h + 1)
                if h >= 2:
                    act.wait_ge(S("at_t"), h - 1)
                for q in (0, 2, 1, 3):
                    bk, c0 = ZB[q]
                    n = (q + 1) * P
                    nc.scalar.activation(pcum[h % 2][:, SEG[q]:SEG[q] + n], bank[bk][:, c0:c0 + n], ACT.Sigmoid,
                                         bias=nbiasbc[:, h:h + 1], scale=-HD ** -0.5)
                for bk, c0, n in ((0, 0, 512), (1, 512, 256), (2, 768, 512)):
                    last = nc.scalar.activation(psig[h % 2][:, c0:c0 + n], bank[bk][:, 0:n], ACT.Sigmoid,
                                                bias=biasbc[:, h:h + 1], scale=HD ** -0.5)
                last.then_inc(S("sig_p"), 1)

            def head_weights(h):
                act.wait_ge(S("at_t"), h + 1)
                if h:
                    act.wait_ge(S("o_p"), h)
                for bk, b0, c0, n in ((3, 0, 0, 512), (4, 0, 512, 512), (1, 256, 1024, 256)):
                    last = nc.scalar.copy(pat[:, c0:c0 + n], bank[bk][:, b0:b0 + n])
                last.then_inc(S("at_out"), 1)

            def value_hi(m):
                act.wait_ge(S(f"v_in{m % VRING}"), 16 * (m // VRING + 1))
                if m >= VHI:
                    act.wait_ge(S("v_used"), m - VHI + 1)
                nc.scalar.copy(vhi[m % VHI][:], vslot[m % VRING][:]).then_inc(S("v_hi"), 1)

            head_sigmoids(0)
            for h in range(EARLY):
                head_sigmoids(h + 1)
                head_weights(h)
            sample_sigmoids(0)
            sample_sigmoids(1)
            head_sigmoids(EARLY + 1)
            sample_sigmoids(2)
            sample_sigmoids(3)
            head_weights(EARLY)
            sample_weights_hi(0)
            sample_weights_hi(1)
            head_sigmoids(EARLY + 2)
            sample_weights_hi(2)
            sample_weights_hi(3)
            head_weights(EARLY + 1)
            for h in range(EARLY + 2, SH):
                n = (h - EARLY - 2) * NPG
                for m in range(4):
                    value_hi(n + m)
                if h + 1 < SH:
                    head_sigmoids(h + 1)
                for m in range(4, NPG):
                    value_hi(n + m)
                    if m == 11:
                        head_weights(h)
            for c in range(2):
                act.wait_ge(S("pt"), 3 + c)
                nc.scalar.copy(pT1_hi[:, c, 0:NP_TOK], bank[4 + c])
                nc.scalar.copy(pT1_hi[:, c, NP_TOK:T], bank[(3, 6)[c]][:, 0:NS]).then_inc(S("pt_hi"), 1)
            act.wait_ge(S("v_used"), NPAGES)
            split_hi(PHASES["up1"][0])
            split_hi(PHASES["up1"][0] + 1)
            split_hi(PHASES["wo1"][0])
            act.wait_ge(S("so1_used"), NS)
            for i in range(KT):
                x_hi(4 * KT + i, g1T[:, i, :])
            for u in range(8):
                j = PHASES["wo1"][0] + u
                split_hi(j + 1)
                act.wait_ge(S("evac"), tiles_through(j))
                x_hi(5 * KT + u, hT[:, u, :])
                square(3 * KT + u, hT[:, u, :])
            for u in range(8):
                j = PHASES["ple1"][0] + u
                split_hi(j + 1)
                if u == 0:
                    rms(3)
                act.wait_ge(S("evac"), tiles_through(j))
                sigmoid_tile(24 + u, work[:, 2 + u % 2, :], work[:, 2 + u % 2, :])
                act.wait_ge(S("h_new"), 8 + u + 1)
                square(4 * KT + u, hT[:, u, :])
            rms(4)
            for k in range(KT):
                act.wait_ge(S("yt_t"), k + 1)
                nc.scalar.copy(ystage[:, :, k * P:(k + 1) * P], bank[4 + k % 2].rearrange("p (b n) -> p b n", b=TB))
                nc.scalar.copy(ysrow[:, k * P:(k + 1) * P], bank[6 + k % 2][0:NS, 0:P]).then_inc(S("y_out"), 1)

        @block.vector
        def _(dve):
            own = Steps(dve, S("dve_steps"))

            def split_lo(j):
                if j >= NJOBS:
                    return
                dve.wait_ge(S("w_hi"), j + 1)
                raw, hi, lo = split_views(j)
                nc.vector.tensor_tensor(lo, raw, hi.bitcast(F32), ALU.subtract).then_inc(S("w_split"), 1)

            def x_lo(n, src):
                dve.wait_ge(S("x_hi"), n + 1)
                hi, lo = x_parts(n)
                nc.vector.tensor_tensor(lo, src, hi.bitcast(F32), ALU.subtract).then_inc(S("x_ready"), 1)

            def halves(ap):
                return ap.rearrange("p (t n) -> p t n", t=2)

            R2 = halves(rstd[:])

            def product_of(j):
                m = tiles_through(j) - 1
                dve.wait_ge(S("mm"), m + 1)
                return pp[m % 2][:, :, 0:H2]

            def normed(j, dst):
                nc.vector.tensor_tensor(halves(dst), product_of(j), R2, ALU.mult).then_inc(S("evac"), 1)

            def recip(i):
                dve.wait_ge(S("r_sqrt"), i + 1)
                own.then(nc.vector.reciprocal(rstd[:], rstd[:]))

            def embed_lo(hi_t, lo_t, c, pbank, sbank):
                nc.vector.tensor_tensor(lo_t[:, c, 0:NP_TOK], pbank, hi_t[:, c, 0:NP_TOK].bitcast(F32), ALU.subtract)
                nc.vector.tensor_tensor(lo_t[:, c, NP_TOK:T], sbank, hi_t[:, c, NP_TOK:T].bitcast(F32),
                                        ALU.subtract).then_inc(S("p_ready"), 1)

            for k in range(KT):
                x_lo(k, hT[:, k, :])
            split_lo(0)
            for c in range(2):
                dve.wait_ge(S("pt_hi"), c + 1)
                embed_lo(pT_hi, pT_lo, c, bank[4 + c], bank[6 + c][:, 64:64 + NS])
            split_lo(1)
            recip(0)
            split_lo(2)
            nc.vector.tensor_tensor(halves(sqacc[0:RANK, :]), product_of(0)[0:RANK], R2[0:RANK],
                                    ALU.mult).then_inc(S("evac"), 1)

            def decay_logits(h):
                dve.wait_ge(S("gk_mm"), h + 1)
                nc.vector.tensor_scalar(halves(gkT[:, h, :]), pp[2 + h % 2][:, :, 0:H2], gcol[:, BGK + h:BGK + h + 1],
                                        None, ALU.add).then_inc(S("gk_out"), 1)

            for h in range(GH):
                j = PHASES["q"][0] + h
                split_lo(j + 1)
                nc.vector.scalar_tensor_tensor(halves(qT[:, h, :]), product_of(j), HK ** -0.5, R2,
                                               ALU.mult, ALU.mult).then_inc(S("evac"), 1)
                if h:
                    decay_logits(h - 1)
            decay_logits(GH - 1)
            for h in range(GH):
                j = PHASES["k"][0] + h
                split_lo(j + 1)
                normed(j, kT[:, h, :])
            for u in range(8):
                j = PHASES["v"][0] + u
                split_lo(j + 1)
                if u >= 2:
                    dve.wait_ge(S("v_t"), u - 1)
                normed(j, work[:, 2 + u % 2, :])
                if u < GH:
                    h = u
                    dve.wait_ge(S("gk_ln"), h + 1)
                    nc.vector.scalar_tensor_tensor(gkT[:, h, NP_TOK:T], gkT[:, h, NP_TOK:T], 0.0, gD[:, h, 0:NS],
                                                   ALU.min, ALU.subtract)
                    own.then(nc.vector.scalar_tensor_tensor(gkT[:, h, 0:NP_TOK], gkT[:, h, 0:NP_TOK], 0.0, gE[:, h, :],
                                                            ALU.min, ALU.subtract))
                    own.then(nc.vector.tensor_tensor_scan(gkT[:, h, 0:NP_TOK], chmask[:], gkT[:, h, 0:NP_TOK], 0.0,
                                                          ALU.mult, ALU.add))
                    chunks = gkT[:, h, 0:NP_TOK].rearrange("p (c n) -> p c n", n=CH)
                    nc.vector.tensor_tensor(gD[:, h, :].rearrange("p (c n) -> p c n", n=CH),
                                            chunks[:, :, CH - 1:CH].to_broadcast([P, NCH, CH]), chunks,
                                            ALU.subtract).then_inc(S("gk_d"), 1)
                else:
                    h = u - GH
                    dve.wait_ge(S("gk_e"), h + 1)
                    nc.vector.tensor_tensor(qT[:, h, 0:NP_TOK], qT[:, h, 0:NP_TOK], gE[:, h, :], ALU.mult)
                    nc.vector.tensor_tensor(gkT[:, h, 0:NP_TOK], gkT[:, h, 0:NP_TOK], kT[:, h, 0:NP_TOK], ALU.mult)
                    nc.vector.tensor_tensor(kT[:, h, 0:NP_TOK], kT[:, h, 0:NP_TOK], gD[:, h, :],
                                            ALU.mult).then_inc(S("kdec"), 1)

            def state_steps(h):
                if h >= 2:
                    dve.wait_ge(S(f"st_out{h % 2}"), 16)
                    dve.wait_ge(S("o_mm"), h - 1)
                for c in range(NCH):
                    kv = chunk_bank(c)
                    if c % 4 == 0:
                        dve.wait_ge(S("kv_mm"), h * NCH + c + 4)
                    if c == 0:
                        ins = nc.vector.tensor_copy(states[:, h % 2, 0, :], kv)
                    else:
                        dve.wait_ge(S("st_step"), h * NCH + c)
                        ins = nc.vector.scalar_tensor_tensor(states[:, h % 2, c, :], states[:, h % 2, c - 1, :],
                                                             dec[:, h, c:c + 1], kv, ALU.mult, ALU.add)
                    ins.then_inc(S("st_step"), 1)

            def gate_o(h):
                dve.wait_ge(S("o_sqrt"), h + 1)
                r = gkT[:, h, 0:NP_TOK]
                own.then(nc.vector.reciprocal(r, r))
                nc.vector.tensor_tensor(qT[:, h, 0:NP_TOK], qT[:, h, 0:NP_TOK], r, ALU.mult)
                own.then(nc.vector.tensor_tensor(kT[:, h, 0:NP_TOK], kT[:, h, 0:NP_TOK], r, ALU.mult))
                for vt, o in enumerate((qT, kT)):
                    g = gT[:, 2 * h + vt, 0:NP_TOK]
                    last = nc.vector.tensor_tensor(g, g, o[:, h, 0:NP_TOK], ALU.mult)
                last.then_inc(S("gated"), 1)

            attm = attmask[:].bitcast(I32).unsqueeze(1).to_broadcast([P, TB, P])
            for u in range(8):
                h = u // 2
                j = PHASES["g"][0] + u
                split_lo(j + 1)
                normed(j, gT[:, u, :])
                dve.wait_ge(S("sigm"), u + 1)
                nc.vector.tensor_tensor(gT[:, u, :], gT[:, u, :], work[:, 2 + u % 2, :], ALU.mult).then_inc(S("silu"), 1)
                if u % 2 == 0:
                    dve.wait_ge(S("att_mm"), h + 1)
                    nc.vector.copy_predicated(attT[:, h, :].rearrange("p (b n) -> p b n", b=TB), attm,
                                              bank[5].rearrange("p (b n) -> p b n", b=TB)).then_inc(S("att_out"), 1)
                else:
                    state_steps(h)
                    if h:
                        gate_o(h - 1)

            def up_tiles(j, dst):
                for c in range(4):
                    m = tiles_through(j) - 4 + c
                    dve.wait_ge(S("mm"), m + 1)
                    nc.vector.tensor_copy(halves(dst[:, (j % 2) * 4 + c, :]), pp[m % 2][:, :, 0:H2]).then_inc(S("evac"), 1)

            def key_row(b):
                if b >= 2:
                    dve.wait_ge(S("skv_mm"), (b - 1) * GH)
                nc.vector.tensor_scalar(krow[:, b % 2, :], k_s[:], ident[0:NS, b:b + 1], None,
                                        ALU.mult).then_inc(S("key_row"), 1)

            krow = attT[0:NS, 0:2, :]
            j = PHASES["up0"][0]
            split_lo(j + 1)
            gate_o(GH - 1)
            dve.wait_ge(S("o_mm"), GH)
            key_row(0)
            key_row(1)
            dve.wait_ge(S("s0_in"), 16)
            for b in range(NS):
                if b >= 2:
                    key_row(b)
                for h in range(GH):
                    n = b * GH + h
                    dve.wait_ge(S("skv_mm"), n + 1)
                    nc.vector.scalar_tensor_tensor(s0[:, n, :], s0[:, n, :], gkT[:, h, NP_TOK + b:NP_TOK + b + 1],
                                                   bank[4 + n % 4][:, 0:HV], ALU.mult, ALU.add).then_inc(S("s_new"), 1)
            dve.wait_ge(S("so_sqrt"), 1)
            own.then(nc.vector.reciprocal(work[:, 3, 32:64], work[:, 3, 0:32]))
            so = work[:, 2, 64:128]
            own.then(nc.vector.tensor_tensor(
                so.rearrange("p (h v b) -> p h v b", h=GH, v=2), bank[4][:, 0:64].rearrange("p (h v b) -> p h v b", h=GH, v=2),
                work[:, 3, 32:64].rearrange("p (h b) -> p h b", h=GH).unsqueeze(2).to_broadcast([P, GH, 2, NS]), ALU.mult))
            nc.vector.tensor_tensor(gT[:, :, NP_TOK:T], gT[:, :, NP_TOK:T], so.rearrange("p (i b) -> p i b", b=NS),
                                    ALU.mult).then_inc(S("so_used"), 1)
            up_tiles(j, up0T)
            split_lo(j + 2)
            up_tiles(j + 1, up0T)
            for i in range(KT):
                x_lo(KT + i, gT[:, i, :])

            def add_residual(j, u):
                nc.vector.tensor_tensor(halves(hT[:, u, :]), product_of(j), halves(hT[:, u, :]), ALU.add).then_inc(S("evac"), 1)

            def add_gated(j, u, up, n):
                g = work[:, 2 + u % 2, :]
                normed(j, g)
                dve.wait_ge(S("sigm"), n + 1)
                own.then(nc.vector.tensor_tensor(g, g, up[:, u, :], ALU.mult))
                nc.vector.tensor_tensor(hT[:, u, :], hT[:, u, :], g, ALU.add).then_inc(S("h_new"), 1)

            for u in range(8):
                j = PHASES["wo0"][0] + u
                split_lo(j + 1)
                add_residual(j, u)
                x_lo(2 * KT + u, hT[:, u, :])
            for u in range(8):
                j = PHASES["ple0"][0] + u
                split_lo(j + 1)
                if u == 0:
                    recip(1)
                add_gated(j, u, up0T, 8 + u)
                x_lo(3 * KT + u, hT[:, u, :])
            for u in range(8):
                j = PHASES["q1"][0] + u
                split_lo(j + 1)
                if u == 0:
                    recip(2)
                normed(j, q1T[:, u, :])
            dve.wait_ge(S("bias_in"), 16)
            nc.vector.tensor_copy(biasrow[0:1, SH:P].rearrange("o (b h) -> o b h", h=SH),
                                  biasrow[0:1, 0:SH].unsqueeze(1).to_broadcast([1, NS - 1, SH])).then_inc(S("bias_row"), 1)

            def score_page(n):
                slot = ring[:, n % RING, :]
                if on_pool(n):
                    dve.wait_ge(S("k_mul_pool"), pool_pages(n + 1))
                else:
                    dve.wait_ge(S("qb_in"), n // NPG + 1)
                    dve.wait_ge(S(f"page_in{n % RING}"), 16 * (n // RING + 1))
                    own.then(nc.vector.tensor_tensor(slot, slot, qb[:, (n // NPG) % 2, :], ALU.mult))
                b = n // NPG
                nc.vector.tensor_reduce(zall[:, n % NPG, b * SH:(b + 1) * SH], slot.rearrange("p (h d) -> p h d", d=HD),
                                        AX.X, ALU.add).then_inc(S("k_used"), 1)

            n = 0
            for i in range(24):
                u = i % 8
                j = PHASES["g1"][0] + i
                if i < 23:
                    split_lo(j + 1)
                if i < 8:
                    normed(j, g1T[:, u, :])
                    dve.wait_ge(S("sigm"), 16 + u + 1)
                    nc.vector.tensor_tensor(g1T[:, u, :], g1T[:, u, :], work[:, 2 + u % 2, :], ALU.mult).then_inc(S("silu"), 1)
                elif i < 16:
                    normed(j, K1T[:, u, :])
                else:
                    if u >= 2:
                        dve.wait_ge(S("kv_t"), 8 + u - 1)
                    normed(j, work[:, 2 + u % 2, :])
                for _ in range(K_PER_JOB):
                    score_page(n)
                    n += 1
            for i in range(2):
                for q in range(TB):
                    c = SEG[q] + (q + 1) * P
                    own.did(nc.vector.memset(pcum[i][:, c:c + 1], 1.0))

            def head_products(h):
                dve.wait_ge(S("sig_p"), h + 1)
                A, C = psig[h % 2], pcum[h % 2]
                for q in range(TB):
                    n, s = (q + 1) * P, SEG[q]
                    rev = C[:, s + n - 1:s - 1:-1] if s else C[:, n - 1::-1]
                    own.did(nc.vector.tensor_tensor_scan(rev, rev, ones[:, 0:1].to_broadcast([P, n]), 1.0,
                                                         ALU.mult, ALU.mult))
                own.wait()
                for q in range(TB):
                    n, s = (q + 1) * P, SEG[q]
                    a = A[:, PSEG[q]:PSEG[q] + n]
                    last = nc.vector.tensor_tensor(a, a, C[:, s + 1:s + n + 1], ALU.mult)
                last.then_inc(S("a_p"), 1)

            def gate_pair(i):
                dve.wait_ge(S("o_p"), 2 * i + 2)
                nc.vector.tensor_tensor(g1T[:, i, 0:NP_TOK], bank[5], g1T[:, i, 0:NP_TOK], ALU.mult).then_inc(S("u1_out"), 1)

            def value_lo(m):
                if m % 8 in POOL_LO:
                    return
                dve.wait_ge(S("v_hi"), m + 1)
                v = vslot[m % VRING]
                nc.vector.tensor_tensor(vlo[m % VRING][:], v[:], vhi[m % VHI][:].bitcast(F32),
                                        ALU.subtract).then_inc(S("v_lo_dve"), 1)

            def sample_rows(b):
                dve.wait_ge(S("v_used"), (b + 1) * NPG)
                if b == 0:
                    dve.wait_ge(S("bmask"), 1)
                nc.vector.tensor_tensor(ob.rearrange("p (t n) -> p t n", t=2), pp[3][:, :, :],
                                        bmask.rearrange("p (t n) -> p t n", t=2), ALU.mult).then_inc(S("ob"), 1)

            def sample_gate(b):
                dve.wait_ge(S("sf_mm"), b + 1)
                nc.vector.tensor_tensor(g1T[:, :, NP_TOK + b], g1T[:, :, NP_TOK + b], bank[6][:, 0:KT],
                                        ALU.mult).then_inc(S("so1_used"), 1)

            def sample_weights_lo(g):
                dve.wait_ge(S("zs_hi"), g + 1)
                nc.vector.tensor_tensor(weight_part(g, 1), bank[6 + g % 2].rearrange("p (j b h) -> p j b h", j=4, b=NS),
                                        weight_part(g, 0).bitcast(F32), ALU.subtract).then_inc(S("zs_lo"), 1)

            head_products(0)
            for h in range(EARLY):
                pages = early_pages(h)
                for n in pages[:len(pages) // 2]:
                    score_page(n)
                head_products(h + 1)
                for n in pages[len(pages) // 2:]:
                    score_page(n)
                if h % 2 == 0 and h:
                    gate_pair(h // 2 - 1)
            nc.vector.memset(scum[:, PAST:PAST + 1], 1.0)
            dve.wait_ge(S("s_sig"), 4)
            own.then(nc.vector.tensor_tensor_scan(scum[:, PAST - 1::-1], scum[:, PAST - 1::-1],
                                                  ones[:, 0:1].to_broadcast([P, PAST]), 1.0, ALU.mult, ALU.mult))
            nc.vector.tensor_tensor(ssig[:], ssig[:], scum[:, 1:PAST + 1], ALU.mult).then_inc(S("a_s"), 1)
            head_products(EARLY + 1)
            if EARLY % 2 == 0:
                gate_pair(EARLY // 2 - 1)
            sample_weights_lo(0)
            sample_weights_lo(1)
            head_products(EARLY + 2)
            sample_weights_lo(2)
            sample_weights_lo(3)
            if EARLY % 2:
                gate_pair(EARLY // 2)
            for h in range(EARLY + 2, SH):
                b = h - EARLY - 2
                if b:
                    sample_rows(b - 1)
                value_lo(b * NPG)
                if b:
                    sample_gate(b - 1)
                for m in range(1, 4):
                    value_lo(b * NPG + m)
                if h + 1 < SH:
                    head_products(h + 1)
                for m in range(4, NPG):
                    value_lo(b * NPG + m)
                if h % 2 == 0:
                    gate_pair(h // 2 - 1)
            gate_pair(SH // 2 - 1)
            sample_rows(NS - 1)
            sample_gate(NS - 1)
            for c in range(2):
                dve.wait_ge(S("pt_hi"), 3 + c)
                embed_lo(pT1_hi, pT1_lo, c, bank[4 + c], bank[(3, 6)[c]][:, 0:NS])
            j = PHASES["up1"][0]
            split_lo(j)
            split_lo(j + 1)
            up_tiles(j, up1T)
            split_lo(j + 2)
            up_tiles(j + 1, up1T)
            for i in range(KT):
                x_lo(4 * KT + i, g1T[:, i, :])
            for u in range(8):
                j = PHASES["wo1"][0] + u
                split_lo(j + 1)
                add_residual(j, u)
                x_lo(5 * KT + u, hT[:, u, :])
            for u in range(8):
                j = PHASES["ple1"][0] + u
                split_lo(j + 1)
                if u == 0:
                    recip(3)
                add_gated(j, u, up1T, 24 + u)
            recip(4)
            for k in range(KT):
                if k >= 2:
                    dve.wait_ge(S("yt_t"), k - 1)
                nc.vector.scalar_tensor_tensor(work[:, 2 + k % 2, :], hT[:, k, :], gcol[:, GFINAL + k:GFINAL + k + 1],
                                               rstd[:], ALU.mult, ALU.mult).then_inc(S("y_t"), 1)

        @block.tensor
        def _(pe):
            pe.wait_ge(S("consts"), 1)
            pe.wait_ge(S("vec_in"), 96)
            nc.tensor.transpose(bank[7][:, 0:NVEC], vrows[:, :], ident[0:NVEC, 0:NVEC]).then_inc(S("gcol_t"), 1)
            pe.wait_ge(S("x_in"), 32)
            pe.wait_ge(S("gcol"), 1)
            for k in range(KT):
                if k >= 2:
                    pe.wait_ge(S("x_hi"), k - 1)
                for b in range(TB):
                    nc.tensor.transpose(bank[4 + k % 2][:, b * P:(b + 1) * P], vtok[:, b, k * P:(k + 1) * P], ident[:])
                nc.tensor.transpose(bank[6 + k % 2][:, 64:64 + NS], vs[:, k * P:(k + 1) * P],
                                    ident[0:NS, 0:NS]).then_inc(S("xt"), 1)
            pe.wait_ge(S("p_in"), 32)
            pe.wait_ge(S("gcol"), 1)
            pe.wait_ge(S("x_hi"), KT)
            for c in range(2):
                for b in range(TB):
                    nc.tensor.transpose(bank[4 + c][:, b * P:(b + 1) * P], gT[:, b, c * P:(c + 1) * P], ident[:])
                nc.tensor.transpose(bank[6 + c][:, 64:64 + NS], ps0[:, c * P:(c + 1) * P],
                                    ident[0:NS, 0:NS]).then_inc(S("pt"), 1)

            def product(j, x0, wait_x=False):
                m = tiles_through(j) - 1
                pe.wait_ge(S("w_split"), j + 1)
                if m >= 2:
                    pe.wait_ge(S("evac"), m - 1)
                _, wh, wl = split_views(j)
                for k in range(KT):
                    if wait_x:
                        pe.wait_ge(S("x_ready"), x0 + k + 1)
                    xh, xl = x_parts(x0 + k)
                    for w, x, first in ((wh, xh, True), (wh, xl, False), (wl, xh, False)):
                        for t in range(2):
                            last = nc.tensor.matmul(pp[m % 2][:, t, 0:H2], w[:, k, :], x[:, t * H2:(t + 1) * H2],
                                                    start=(k == 0 and first), stop=(k == KT - 1 and w is wl))
                last.then_inc(S("mm"), 1)

            def up_product(j, p_hi, p_lo, n):
                pe.wait_ge(S("w_split"), j + 1)
                pe.wait_ge(S("p_ready"), n)
                _, wh, wl = split_views(j)
                for c in range(4):
                    m = tiles_through(j) - 4 + c
                    pe.wait_ge(S("evac"), m - 1)
                    for k in range(2):
                        for w, x, first in ((wh, p_hi, True), (wh, p_lo, False), (wl, p_hi, False)):
                            for t in range(2):
                                last = nc.tensor.matmul(pp[m % 2][:, t, 0:H2], w[:, k, c * P:(c + 1) * P],
                                                        x[:, k, t * H2:(t + 1) * H2],
                                                        start=(k == 0 and first), stop=(k == 1 and w is wl))
                    last.then_inc(S("mm"), 1)

            def square_sum(i):
                pe.wait_ge(S("sq_added"), KT * (i + 1))
                for t in range(2):
                    last = nc.tensor.matmul(pp[3][:, t, 0:H2], ones[:], sqacc[:, t * H2:(t + 1) * H2],
                                            start=True, stop=True)
                last.then_inc(S("ss_mm"), 1)

            def token_major(src, b0, done):
                for b in range(TB):
                    nc.tensor.transpose(bank[b0][:, b * P:(b + 1) * P], src[:, b * P:(b + 1) * P], ident[:])
                nc.tensor.transpose(bank[b0 + 1][0:NS, 0:P], src[:, NP_TOK:T], ident[:]).then_inc(done, 1)

            product(0, 0, wait_x=True)
            pe.wait_ge(S("p_ready"), 2)
            square_sum(0)
            pe.wait_ge(S("w2_in"), 16)
            for h in range(GH):
                product(PHASES["q"][0] + h, 0)
                if h == 0:
                    pe.wait_ge(S("evac"), 1)
                if h >= 2:
                    pe.wait_ge(S("gk_out"), h - 1)
                for t in range(2):
                    last = nc.tensor.matmul(pp[2 + h % 2][:, t, 0:H2], w2[:, h * P:(h + 1) * P],
                                            sqacc[0:RANK, t * H2:(t + 1) * H2], start=True, stop=True)
                last.then_inc(S("gk_mm"), 1)
            for h in range(GH):
                product(PHASES["k"][0] + h, 0)

            def v_tile(u):
                pe.wait_ge(S("evac"), PHASES["v"][2] + u + 1)
                pe.wait_ge(S("v_out"), u) if u else pe.wait_ge(S("ks_out"), 1)
                token_major(work[:, 2 + u % 2, :], 4, S("v_t"))

            for u in range(8):
                product(PHASES["v"][0] + u, 0)
                if u == 0:
                    pe.wait_ge(S("evac"), last_tile("k"))
                    for h in range(GH):
                        last = nc.tensor.transpose(bank[4][0:NS, h * P:(h + 1) * P], kT[:, h, NP_TOK:T], ident[:])
                    last.then_inc(S("ks_t"), 1)
                else:
                    v_tile(u - 1)

            def gla_scores(h):
                pe.wait_ge(S("kdec"), h + 1)
                if h == 0:
                    pe.wait_ge(S("v_out"), 8)
                if h >= 2:
                    pe.wait_ge(S("o_sqrt"), h - 1)
                for b in range(TB):
                    last = nc.tensor.transpose(bank[4][:, b * P:(b + 1) * P], kT[:, h, b * P:(b + 1) * P], ident[:])
                last.then_inc(S("kd_t"), 1)
                if h:
                    pe.wait_ge(S("att_out"), h)
                for b in range(TB):
                    last = nc.tensor.matmul(bank[5][:, b * P:(b + 1) * P], gkT[:, h, b * P:(b + 1) * P],
                                            qT[:, h, b * P:(b + 1) * P], start=True, stop=True)
                last.then_inc(S("att_mm"), 1)

            def gla_states(h):
                pe.wait_ge(S("kd_out"), h + 1)
                if h:
                    pe.wait_ge(S("o_out"), h)
                for c in range(NCH):
                    if c == 4:
                        pe.wait_ge(S("st_step"), h * NCH + 4)
                    r = (c % 2) * CH
                    nc.tensor.matmul(chunk_bank(c), kdtok[r:r + CH, h, c // 2, :], vtok[r:r + CH, c // 2, h * HV:(h + 1) * HV],
                                     start=True, stop=True).then_inc(S("kv_mm"), 1)

            def gla_output(h):
                pe.wait_ge(S("att_out"), h + 1)
                pe.wait_ge(S("st_step"), (h + 1) * NCH)
                for vt in range(2):
                    for b in range(TB):
                        nc.tensor.matmul(bank[6 + vt][:, b * P:(b + 1) * P],
                                         vtok[:, b, h * HV + vt * P:h * HV + (vt + 1) * P],
                                         attT[:, h, b * P:(b + 1) * P], start=(b == 0), stop=False, skip_group_check=True)
                    for c in range(1, NCH):
                        last = nc.tensor.matmul(bank[6 + vt][:, c * CH:(c + 1) * CH],
                                                states[:, h % 2, c - 1, vt * P:(vt + 1) * P],
                                                qT[:, h, c * CH:(c + 1) * CH], start=False, stop=(c == NCH - 1),
                                                skip_group_check=True)
                last.then_inc(S("o_mm"), 1)

            def gla_square_sum(h):
                pe.wait_ge(S("o_out"), h + 1)
                pe.wait_ge(S("kd_out"), min(h + 2, GH))
                for vt in range(2):
                    last = nc.tensor.matmul(bank[4], ones[:], work[:, vt, 0:NP_TOK], start=(vt == 0), stop=(vt == 1))
                last.then_inc(S("oss_mm"), 1)

            for u in range(8):
                h = u // 2
                product(PHASES["g"][0] + u, 0)
                if u == 0:
                    v_tile(7)
                if u % 2 == 0:
                    if h:
                        gla_output(h - 1)
                    gla_scores(h)
                else:
                    if h:
                        gla_square_sum(h - 1)
                    gla_states(h)
            gla_output(GH - 1)
            gla_square_sum(GH - 1)
            pe.wait_ge(S("o_sqrt"), GH)
            for n in range(NS * GH):
                h = n % GH
                pe.wait_ge(S("key_row"), n // GH + 1)
                if n >= 4:
                    pe.wait_ge(S("s_new"), n - 3)
                nc.tensor.matmul(bank[4 + n % 4][:, 0:HV], attT[0:NS, (n // GH) % 2, h * P:(h + 1) * P],
                                 vs[:, h * HV:(h + 1) * HV], start=True, stop=True).then_inc(S("skv_mm"), 1)
            pe.wait_ge(S("s_new"), NS * GH)
            for h in range(GH):
                for vt in range(2):
                    for b in range(NS):
                        c = (2 * h + vt) * NS + b
                        last = nc.tensor.matmul(bank[4][:, c:c + 1], s0[:, b * GH + h, vt * P:(vt + 1) * P],
                                                qT[:, h, NP_TOK + b:NP_TOK + b + 1], start=True, stop=True)
            last.then_inc(S("so_mm"), 1)
            pe.wait_ge(S("sosq"), 1)
            for vt in range(2):
                last = nc.tensor.matmul(bank[5][:, 0:GH * NS], ones[:],
                                        work[:, 2, 0:2 * GH * NS].rearrange("p (h v b) -> p v h b", h=GH, v=2)[:, vt],
                                        start=(vt == 0), stop=(vt == 1))
            last.then_inc(S("soss_mm"), 1)
            for u in range(2):
                up_product(PHASES["up0"][0] + u, pT_hi, pT_lo, 2)
            for u in range(8):
                product(PHASES["wo0"][0] + u, KT, wait_x=(u == 0))
            for u in range(8):
                product(PHASES["ple0"][0] + u, 2 * KT, wait_x=(u == 0))
                if u == 0:
                    square_sum(1)
            for u in range(8):
                product(PHASES["q1"][0] + u, 3 * KT, wait_x=(u == 0))
                if u == 0:
                    square_sum(2)
            pe.wait_ge(S("evac"), last_tile("q1"))
            for k in range(KT):
                last = nc.tensor.transpose(bank[4 + k // 4][0:NS, (k % 4) * P:(k % 4 + 1) * P], q1T[:, k, NP_TOK:T], ident[:])
            last.then_inc(S("qs_t"), 1)
            pe.wait_ge(S("qs_out"), 1)
            pe.wait_ge(S("bias_row"), 1)
            nc.tensor.matmul(bank[4][:, 0:SH], ones[0:1, :], biasrow[0:1, 0:SH], start=True, stop=True)
            nc.tensor.matmul(bank[5][:, 0:1], biasrow[0:1, :], ones[0:1, 0:1], start=True, stop=True).then_inc(S("bias_mm"), 1)

            def query_everywhere(b):
                if b:
                    pe.wait_ge(S("qb_in"), b)
                for t in range(2):
                    last = nc.tensor.matmul(pp[3][:, t, :], sel[:, b, :], work[0:NS, t, 0:512], start=True, stop=True)
                last.then_inc(S("qb_mm"), 1)

            pe.wait_ge(S("sel"), 1)
            query_everywhere(0)
            query_everywhere(1)
            asked = 2

            def kv_transposes(t):
                pe.wait_ge(S("evac"), PHASES["K"][2] + t + 1)
                pe.wait_ge(S("kv_out"), t) if t else pe.wait_ge(S("bias_out"), 1)
                token_major(K1T[:, t, :] if t < 8 else work[:, 2 + t % 2, :], 4, S("kv_t"))

            for i in range(24):
                product(PHASES["g1"][0] + i, 3 * KT)
                while asked < NS and asked <= (i * K_PER_JOB) // NPG + 1 and i >= 1:
                    query_everywhere(asked)
                    asked += 1
                if i >= KV_LAG + 8:
                    kv_transposes(i - KV_LAG - 8)
            while asked < NS:
                query_everywhere(asked)
                asked += 1
            for t in range(16 - KV_LAG, 16):
                kv_transposes(t)
            def sample_scores_back(g):
                if g == 0:
                    pe.wait_ge(S("k_used"), NPAGES)
                    pe.wait_ge(S("qb_in"), NS)
                if g >= 2:
                    pe.wait_ge(S("s_sig"), g - 1)
                for c in range(4):
                    last = nc.tensor.transpose(bank[6 + g % 2][:, c * P:(c + 1) * P], zall[:, g * 4 + c, :], ident[:])
                last.then_inc(S("z_t"), 1)

            def sample_weights_back(g):
                if g == 0:
                    pe.wait_ge(S("a_s"), 1)
                if g >= 2:
                    pe.wait_ge(S("zs_lo"), g - 1)
                for c in range(4):
                    j = g * 4 + c
                    last = nc.tensor.transpose(bank[6 + g % 2][:, c * P:(c + 1) * P], ssig[:, j * P:(j + 1) * P], ident[:])
                last.then_inc(S("a_t"), 1)

            def scores(h):
                i, r = h // 2, (h % 2) * HD
                if h:
                    pe.wait_ge(S("sig_p"), h)
                for q in (0, 2, 1, 3):
                    bk, c0 = ZB[q]
                    n = (q + 1) * P
                    nc.tensor.matmul(bank[bk][:, c0:c0 + n], q1T[r:r + HD, i, q * P:(q + 1) * P],
                                     K1T[r:r + HD, i, 0:n], start=True, stop=False, skip_group_check=True)
                    last = nc.tensor.matmul(bank[bk][:, c0 + n - P:c0 + n], identb[:], maskneg[:],
                                            start=False, stop=True, skip_group_check=True)
                last.then_inc(S("z_p"), 1)

            def weights_back(h):
                pe.wait_ge(S("a_p"), h + 1)
                if h:
                    pe.wait_ge(S("at_out"), h)
                pe.wait_ge(S("sig_p"), min(h + 2, SH))
                for kb in range(TB):
                    bk, c0 = AB[kb]
                    for q in range(kb, TB):
                        last = nc.tensor.transpose(bank[bk][:, c0 + (q - kb) * P:c0 + (q - kb + 1) * P],
                                                   psig[h % 2][:, PSEG[q] + kb * P:PSEG[q] + (kb + 1) * P], ident[:])
                last.then_inc(S("at_t"), 1)

            def values(h):
                r = (h % 2) * HD
                pe.wait_ge(S("at_out"), h + 1)
                if h >= 2 and h % 2 == 0:
                    pe.wait_ge(S("u1_out"), h // 2)
                for kb in range(TB):
                    n = (TB - kb) * P
                    last = nc.tensor.matmul(bank[5][r:r + HD, kb * P:NP_TOK], V1[:, kb, h * HD:(h + 1) * HD],
                                            pat[:, AO[kb]:AO[kb] + n], start=(kb == 0), stop=(kb == TB - 1),
                                            skip_group_check=True)
                last.then_inc(S("o_p"), 1)

            def value_page(m):
                b, j = m // NPG, m % NPG
                if m % 8 in POOL_LO:
                    pe.wait_ge(S("v_lo_pool"), pool_lo(m + 1))
                else:
                    pe.wait_ge(S("v_lo_dve"), m + 1 - pool_lo(m + 1))
                if j == 0 and b:
                    pe.wait_ge(S("so1_used"), b)
                c = 2 * (j * P + b * SH)
                for part, v in enumerate((vhi[m % VHI][:], vlo[m % VRING][:])):
                    for t in range(2):
                        last = nc.tensor.matmul(pp[3][:, t, :], zs[:, c:c + P], v[:, t * 512:(t + 1) * 512],
                                                start=(j == 0 and part == 0), stop=(j == NPG - 1 and part == 1))
                last.then_inc(S("v_used"), 1)

            def sample_features(b):
                pe.wait_ge(S("ob"), b + 1)
                for i in range(KT):
                    last = nc.tensor.matmul(bank[6][:, i:i + 1], ob[:, i * P:(i + 1) * P], ones[:, 0:1], start=True, stop=True)
                last.then_inc(S("sf_mm"), 1)

            scores(0)
            pe.wait_ge(S("kv_out"), 16)
            for h in range(EARLY):
                scores(h + 1)
                weights_back(h)
                values(h)
            sample_scores_back(0)
            sample_scores_back(1)
            scores(EARLY + 1)
            sample_scores_back(2)
            sample_scores_back(3)
            weights_back(EARLY)
            values(EARLY)
            sample_weights_back(0)
            sample_weights_back(1)
            scores(EARLY + 2)
            sample_weights_back(2)
            sample_weights_back(3)
            weights_back(EARLY + 1)
            values(EARLY + 1)
            pe.wait_ge(S("zs_lo"), 4)
            pe.wait_ge(S("zs_pad"), 1)
            for h in range(EARLY + 2, SH):
                b = h - EARLY - 2
                if h + 1 < SH:
                    scores(h + 1)
                if b:
                    sample_features(b - 1)
                for m in range(NPG // 2):
                    value_page(b * NPG + m)
                weights_back(h)
                for m in range(NPG // 2, NPG):
                    value_page(b * NPG + m)
                values(h)
            sample_features(NS - 1)
            pe.wait_ge(S("so1_used"), NS)
            pe.wait_ge(S("p1_in"), 32)
            pe.wait_ge(S("u1_out"), KT)
            for c in range(2):
                for b in range(TB):
                    nc.tensor.transpose(bank[4 + c][:, b * P:(b + 1) * P], pin1[:, b, c * P:(c + 1) * P], ident[:])
                nc.tensor.transpose(bank[(3, 6)[c]][:, 0:NS], ps1[:, c * P:(c + 1) * P],
                                    ident[0:NS, 0:NS]).then_inc(S("pt"), 1)
            for u in range(2):
                up_product(PHASES["up1"][0] + u, pT1_hi, pT1_lo, 4)
            for u in range(8):
                product(PHASES["wo1"][0] + u, 4 * KT, wait_x=(u == 0))
            for u in range(8):
                product(PHASES["ple1"][0] + u, 5 * KT, wait_x=(u == 0))
                if u == 0:
                    square_sum(3)
            square_sum(4)
            for k in range(KT):
                pe.wait_ge(S("y_t"), k + 1)
                if k >= 2:
                    pe.wait_ge(S("y_out"), k - 1)
                src = work[:, 2 + k % 2, :]
                for b in range(TB):
                    nc.tensor.transpose(bank[4 + k % 2][:, b * P:(b + 1) * P], src[:, b * P:(b + 1) * P], ident[:])
                nc.tensor.transpose(bank[6 + k % 2][0:NS, 0:P], src[:, NP_TOK:T], ident[:]).then_inc(S("yt_t"), 1)


KV_LAG = 1

_INS = ['x_prompt', 'x_sample', 'state_gla', 'cache_k', 'cache_v', 'page_table', 'p_prompt', 'p_sample',
        'g_pre', 'w_ple_gate', 'w_ple_up', 'g_ple', 'gla_w_in', 'gla_w_gk2', 'gla_b_gk', 'gla_g_out', 'gla_w_out',
        'g_kv', 'w_kv', 'sb_w_in', 'sb_bias', 'sb_w_out', 'g_final']
_OUTS = [(1, 512, 1024), (8, 1, 1024), (1, 1, 4, 128, 256), (1, 8, 4, 128, 256),
         (1, 512, 16, 64), (1, 512, 16, 64), (8, 1, 16, 64), (8, 1, 16, 64)]


def kernel(**inputs):
    import numpy as _np
    import concourse.bacc as _bacc
    from concourse import mybir as _mybir
    from concourse.bass_utils import run_bass_kernel_spmd as _run

    nc = _bacc.Bacc("TRN2", target_bir_lowering=False, num_devices=1)
    arrays, args = {}, []
    for name in _INS:
        a = _np.ascontiguousarray(inputs[name])
        arrays[f"in_{name}_dram"] = a
        args.append(nc.dram_tensor(f"in_{name}_dram", a.shape, _mybir.dt.from_np(a.dtype), kind="ExternalInput").ap())
    for i, shape in enumerate(_OUTS):
        args.append(nc.dram_tensor(f"out_{i}_dram", shape, F32, kind="ExternalOutput").ap())
    build(nc, *args)
    r = _run(nc, [arrays], core_ids=[0])
    return tuple(r.results[0][f"out_{i}_dram"] for i in range(len(_OUTS)))
```
